# Optimizing a Trainium2 kernel written in Bass

```python
import jax, jax.numpy as jnp
from jax import lax
import numpy as np

D_MODEL = 1024
BATCH = 1
SEQ = 1024
DEPTH = 1
DEC_BATCH = 8
DEC_SEQ = 1
PAST_LEN = 1024
PAGE_SIZE = 128

HEAD_DIM = 64
MIX_W = D_MODEL
RET_W = MIX_W // 2
ATT_W = MIX_W - RET_W
H_RET = RET_W // HEAD_DIM
H_ATT = ATT_W // HEAD_DIM
PROJ_SPLITS = [RET_W, 2 * RET_W, 3 * RET_W, 4 * RET_W, 4 * RET_W + ATT_W, 4 * RET_W + 2 * ATT_W]
N_PROJ = 4 * RET_W + 3 * ATT_W
RET_CHUNK = 128
DIL_BRANCHES = ((128, 1), (512, 4), (2048, 16))
MAX_WINDOW = 2048
N_KEYS = 128
N_EXPERTS = N_KEYS * N_KEYS
PEER_HEADS = 8
PEER_QDIM = 128
PEER_HALF = PEER_QDIM // 2
PEER_TOPK = 16
PEER_BLOCK = 128
EPS = 1e-6
F32 = jnp.float32

kernel_name = "hymba_retention_dilated_peer_step"

def rmsnorm(x, g):
    xf = x.astype(F32)
    y = xf * lax.rsqrt(jnp.mean(xf * xf, -1, keepdims=True) + EPS) * g.astype(F32)
    return y.astype(x.dtype)

def head_rmsnorm(x, g):
    xf = x.astype(F32)
    y = xf * lax.rsqrt(jnp.mean(xf * xf, -1, keepdims=True) + EPS) * g.astype(F32)
    return y.astype(x.dtype)

def head_groupnorm(o, g):
    of = o.astype(F32)
    mu = jnp.mean(of, -1, keepdims=True)
    var = jnp.mean(jnp.square(of - mu), -1, keepdims=True)
    return (of - mu) * lax.rsqrt(var + EPS) * g.astype(F32)

def ret_log_decay():
    return jnp.log1p(-jnp.exp2(-5.0 - jnp.arange(H_RET, dtype=F32)))

def alibi_slopes():
    return jnp.exp2(-8.0 * (jnp.arange(H_ATT, dtype=F32) + 1.0) / H_ATT)

def retention(q, k, v, s0):
    B, L, H, dh = q.shape
    cs = RET_CHUNK if L % RET_CHUNK == 0 else L
    nc = L // cs
    lg = ret_log_decay()
    qc = q.reshape(B, nc, cs, H, dh).astype(F32)
    kc = k.reshape(B, nc, cs, H, dh).astype(F32)
    vc = v.reshape(B, nc, cs, H, dh).astype(F32)
    i = jnp.arange(cs)
    diff = i[:, None] - i[None, :]
    intra = jnp.where(diff >= 0, jnp.exp(jnp.maximum(diff, 0)[None].astype(F32) * lg[:, None, None]), 0.0)
    scores = jnp.einsum('bnihd,bnjhd->bnhij', qc, kc) * intra[None, None]
    o_intra = jnp.einsum('bnhij,bnjhe->bnihe', scores, vc)
    w_end = jnp.exp((cs - 1 - i)[None, :].astype(F32) * lg[:, None])
    kv_chunk = jnp.einsum('bnjhd,hj,bnjhe->bnhde', kc, w_end, vc)
    chunk_decay = jnp.exp(cs * lg)[None, :, None, None]

    def step(s, kv):
        return chunk_decay * s + kv, s

    s_fin, s_starts = lax.scan(step, s0, jnp.moveaxis(kv_chunk, 1, 0))
    s_starts = jnp.moveaxis(s_starts, 0, 1)
    w_start = jnp.exp((i + 1)[None, :].astype(F32) * lg[:, None])
    o_inter = jnp.einsum('bnihd,hi,bnhde->bnihe', qc, w_start, s_starts)
    return (o_intra + o_inter).reshape(B, L, H, dh), s_fin

def dilated_branch_prompt(q, k, v, window, dil):
    B, S, H, hd = q.shape
    nw = window // dil
    M = S // dil
    nb = -(-M // nw)
    Mp = nb * nw

    def to_res(x):
        x = x.reshape(B, M, dil, H, hd).transpose(0, 2, 1, 3, 4).astype(F32)
        x = jnp.pad(x, ((0, 0), (0, 0), (0, Mp - M), (0, 0), (0, 0)))
        return x.reshape(B, dil, nb, nw, H, hd)

    def with_prev(x):
        prev = jnp.pad(x, ((0, 0), (0, 0), (1, 0), (0, 0), (0, 0), (0, 0)))[:, :, :-1]
        return jnp.concatenate([prev, x], axis=3)

    qb = to_res(q)
    kk = with_prev(to_res(k))
    vv = with_prev(to_res(v))
    s = jnp.einsum('brnihd,brnjhd->brnhij', qb, kk) * (hd ** -0.5)
    ii = jnp.arange(nw)[:, None]
    jj = jnp.arange(2 * nw)[None, :]
    off = ii + nw - jj
    band = (off >= 0) & (off <= nw)
    blk = jnp.arange(nb)[:, None, None]
    valid = band[None] & (blk * nw + jj[None] - nw >= 0)
    bias = -alibi_slopes()[:, None, None] * (off * dil).astype(F32)[None]
    s = jnp.where(valid[None, None, :, None], s + bias[None, None, None], -jnp.inf)
    m = jnp.max(s, -1, keepdims=True)
    p = jnp.exp(s - m)
    den = jnp.sum(p, -1)
    o = jnp.einsum('brnhij,brnjhd->brnihd', p, vv) / den.transpose(0, 1, 2, 4, 3)[..., None]
    lse = (m[..., 0] + jnp.log(den)).transpose(0, 1, 2, 4, 3)
    o = o.reshape(B, dil, Mp, H, hd)[:, :, :M].transpose(0, 2, 1, 3, 4).reshape(B, S, H, hd)
    lse = lse.reshape(B, dil, Mp, H)[:, :, :M].transpose(0, 2, 1, 3).reshape(B, S, H)
    return o, lse

def merge_branches(outs, lses):
    w = jax.nn.softmax(jnp.stack(lses), axis=0)
    return jnp.sum(w[..., None] * jnp.stack(outs), axis=0)

def dilated_attention_prompt(q, k, v):
    outs, lses = [], []
    for window, dil in DIL_BRANCHES:
        o, lse = dilated_branch_prompt(q, k, v, window, dil)
        outs.append(o)
        lses.append(lse)
    return merge_branches(outs, lses)

def dilated_attention_sample(q, k_new, v_new, win_k, win_v):
    WIN = win_k.shape[1]
    T = q.shape[1]
    hd = q.shape[-1]
    kk = jnp.concatenate([win_k, k_new.astype(win_k.dtype)], axis=1).astype(F32)
    vv = jnp.concatenate([win_v, v_new.astype(win_v.dtype)], axis=1).astype(F32)
    qf = q.astype(F32)
    t = jnp.arange(T)
    outs, lses = [], []
    for window, dil in DIL_BRANCHES:
        nw = window // dil
        jj = jnp.arange(nw + 1)
        idx = WIN + t[:, None] - jj[None, :] * dil
        ok = idx >= 0
        idx_c = jnp.maximum(idx, 0)
        kg = kk[:, idx_c]
        vg = vv[:, idx_c]
        s = jnp.einsum('bthd,btjhd->bhtj', qf, kg) * (hd ** -0.5)
        s = s - alibi_slopes()[:, None, None] * (jj * dil).astype(F32)[None, None, :]
        s = jnp.where(ok[None, None], s, -jnp.inf)
        lse = jax.nn.logsumexp(s, axis=-1)
        p = jnp.exp(s - lse[..., None])
        outs.append(jnp.einsum('bhtj,btjhd->bthd', p, vg))
        lses.append(lse.transpose(0, 2, 1))
    return merge_branches(outs, lses)

def peer(xn, w_pq, sub_keys, peer_u, peer_v):
    N, D = xn.shape
    Np = -(-N // PEER_BLOCK) * PEER_BLOCK
    xp = jnp.pad(xn, ((0, Np - N), (0, 0)))

    def block(xb):
        qh = (xb @ w_pq).reshape(PEER_BLOCK, PEER_HEADS, 2, PEER_HALF)
        sc = jnp.einsum('thcq,hckq->thck', qh, sub_keys).astype(F32)
        s1, i1 = lax.top_k(sc[:, :, 0], PEER_TOPK)
        s2, i2 = lax.top_k(sc[:, :, 1], PEER_TOPK)
        cand = (s1[..., :, None] + s2[..., None, :]).reshape(PEER_BLOCK, PEER_HEADS, PEER_TOPK * PEER_TOPK)
        cidx = (i1[..., :, None] * N_KEYS + i2[..., None, :]).reshape(PEER_BLOCK, PEER_HEADS, PEER_TOPK * PEER_TOPK)
        top_s, top_pos = lax.top_k(cand, PEER_TOPK)
        eidx = jnp.take_along_axis(cidx, top_pos, axis=-1)
        g = jax.nn.softmax(top_s, axis=-1)
        u = jnp.take(peer_u, eidx, axis=0)
        a = jax.nn.gelu(jnp.einsum('thkd,td->thk', u, xb).astype(F32), approximate=False)
        vsel = jnp.take(peer_v, eidx, axis=0)
        return jnp.einsum('thk,thkd->td', (g * a).astype(xb.dtype), vsel)

    y = lax.map(block, xp.reshape(Np // PEER_BLOCK, PEER_BLOCK, D))
    return y.reshape(Np, D)[:N]

def adaln(c, w_ada, b_ada):
    mod = jax.nn.silu(c) @ w_ada + b_ada
    return jnp.split(mod[:, None, :], 6, axis=-1)

def mixer_projections(h, w_in, g_qn, g_kn):
    Bx, L, _ = h.shape
    parts = jnp.split(h @ w_in, PROJ_SPLITS, axis=-1)
    rq, rk, rv, rg, aq, ak, av = [p.reshape(Bx, L, -1, HEAD_DIM) for p in parts]
    return rq, rk * (HEAD_DIM ** -0.5), rv, rg, head_rmsnorm(aq, g_qn), head_rmsnorm(ak, g_kn), av

def mixer_output(o_ret, rg, o_att, g_ret, w_out):
    Bx, L = rg.shape[:2]
    ret = (head_groupnorm(o_ret, g_ret) * jax.nn.silu(rg.astype(F32))).astype(rg.dtype)
    mix = jnp.concatenate([ret, o_att.astype(rg.dtype)], axis=-1).reshape(Bx, L, MIX_W)
    return mix @ w_out

def layer(x, c, core, lw):
    (w_ada, b_ada, g_norm1, w_in, g_qn, g_kn, g_ret, w_out, g_norm2, w_pq, sub_keys, peer_u, peer_v) = lw
    sh1, sc1, gt1, sh2, sc2, gt2 = adaln(c, w_ada, b_ada)
    h = rmsnorm(x, g_norm1) * (1 + sc1) + sh1
    rq, rk, rv, rg, aq, ak, av = mixer_projections(h, w_in, g_qn, g_kn)
    o_ret, o_att, state = core(rq, rk, rv, aq, ak, av)
    x = x + gt1 * mixer_output(o_ret, rg, o_att, g_ret, w_out)
    h2 = rmsnorm(x, g_norm2) * (1 + sc2) + sh2
    Bx, L, D = x.shape
    x = x + gt2 * peer(h2.reshape(Bx * L, D), w_pq, sub_keys, peer_u, peer_v).reshape(Bx, L, D)
    return x, state

def prompt_core(rq, rk, rv, aq, ak, av):
    Bx, L = rq.shape[:2]
    s0 = jnp.zeros((Bx, H_RET, HEAD_DIM, HEAD_DIM), F32)
    o_ret, s_fin = retention(rq, rk, rv, s0)
    o_att = dilated_attention_prompt(aq, ak, av)
    keep = min(MAX_WINDOW, L)
    return o_ret, o_att, (s_fin, ak[:, L - keep:], av[:, L - keep:])

def make_sample_core(s_ret, win_k, win_v):
    def core(rq, rk, rv, aq, ak, av):
        o_ret, s_new = retention(rq, rk, rv, s_ret.astype(F32))
        o_att = dilated_attention_sample(aq, ak, av, win_k, win_v)
        return o_ret, o_att, (s_new, ak, av)
    return core

def setup_inputs(seed: int = 0) -> dict:
    key = jax.random.key(seed)
    ks = jax.random.split(key, 20)
    win = min(MAX_WINDOW, PAST_LEN)

    def nrm(k, shape, s):
        return jax.random.normal(k, shape, F32) * s

    return {
        "x_prompt": nrm(ks[0], (BATCH, SEQ, D_MODEL), 1.0),
        "x_sample": nrm(ks[1], (DEC_BATCH, DEC_SEQ, D_MODEL), 1.0),
        "c_prompt": nrm(ks[2], (BATCH, D_MODEL), 1.0),
        "c_sample": nrm(ks[3], (DEC_BATCH, D_MODEL), 1.0),
        "state_ret": nrm(ks[4], (DEPTH, DEC_BATCH, H_RET, HEAD_DIM, HEAD_DIM), 0.5),
        "cache_win_k": nrm(ks[5], (DEPTH, DEC_BATCH, win, H_ATT, HEAD_DIM), 1.0),
        "cache_win_v": nrm(ks[6], (DEPTH, DEC_BATCH, win, H_ATT, HEAD_DIM), 1.0),
        "w_ada": nrm(ks[7], (DEPTH, D_MODEL, 6 * D_MODEL), 0.5 * D_MODEL ** -0.5),
        "b_ada": nrm(ks[8], (DEPTH, 6 * D_MODEL), 0.02),
        "g_norm1": 1.0 + nrm(ks[9], (DEPTH, D_MODEL), 0.02),
        "w_in": nrm(ks[10], (DEPTH, D_MODEL, N_PROJ), D_MODEL ** -0.5),
        "g_qn": 1.0 + nrm(ks[11], (DEPTH, H_ATT, HEAD_DIM), 0.02),
        "g_kn": 1.0 + nrm(ks[12], (DEPTH, H_ATT, HEAD_DIM), 0.02),
        "g_ret": 1.0 + nrm(ks[13], (DEPTH, H_RET, HEAD_DIM), 0.02),
        "w_out": nrm(ks[14], (DEPTH, MIX_W, D_MODEL), MIX_W ** -0.5),
        "g_norm2": 1.0 + nrm(ks[15], (DEPTH, D_MODEL), 0.02),
        "w_pq": nrm(ks[16], (DEPTH, D_MODEL, PEER_HEADS * PEER_QDIM), D_MODEL ** -0.5),
        "sub_keys": nrm(ks[17], (DEPTH, PEER_HEADS, 2, N_KEYS, PEER_HALF), PEER_HALF ** -0.5),
        "peer_u": nrm(ks[18], (DEPTH, N_EXPERTS, D_MODEL), D_MODEL ** -0.5),
        "peer_v": nrm(ks[19], (DEPTH, N_EXPERTS, D_MODEL), PEER_HEADS ** -0.5),
    }

def reference(x_prompt, x_sample, c_prompt, c_sample, state_ret, cache_win_k, cache_win_v,
              w_ada, b_ada, g_norm1, w_in, g_qn, g_kn, g_ret, w_out, g_norm2,
              w_pq, sub_keys, peer_u, peer_v):
    y_p = x_prompt
    y_s = x_sample
    ret_p, wk_p, wv_p, ret_s, wk_s, wv_s = [], [], [], [], [], []
    for l in range(DEPTH):
        lw = (w_ada[l], b_ada[l], g_norm1[l], w_in[l], g_qn[l], g_kn[l], g_ret[l], w_out[l],
              g_norm2[l], w_pq[l], sub_keys[l], peer_u[l], peer_v[l])
        y_p, (sp, kp, vp) = layer(y_p, c_prompt, prompt_core, lw)
        y_s, (ss, ks_, vs_) = layer(y_s, c_sample, make_sample_core(state_ret[l], cache_win_k[l], cache_win_v[l]), lw)
        ret_p.append(sp); wk_p.append(kp); wv_p.append(vp)
        ret_s.append(ss); wk_s.append(ks_); wv_s.append(vs_)
    new_ret_p = jnp.stack(ret_p)
    new_wk_p = jnp.stack(wk_p)
    new_wv_p = jnp.stack(wv_p)
    new_ret_s = jnp.stack(ret_s)
    new_wk_s = jnp.stack(wk_s)
    new_wv_s = jnp.stack(wv_s)
    return (y_p, y_s, new_ret_p, new_wk_p, new_wv_p, new_ret_s, new_wk_s, new_wv_s)


_drawn_inputs = setup_inputs


def setup_inputs(seed=0):
    import zlib

    import numpy as np

    out = dict(_drawn_inputs(seed))
    spreads = {}
    factors = {'g_norm1': 2.92, 'g_qn': 24.403, 'g_kn': 8.238, 'g_ret': 8.0, 'g_norm2': 22.192}
    for name, (base, spread) in spreads.items():
        noise = np.random.default_rng([zlib.crc32(name.encode()), seed]).standard_normal(out[name].shape)
        drawn = base * np.exp(spread * noise) if base else spread * noise
        out[name] = __import__('jax').numpy.asarray(drawn.astype(out[name].dtype))
    for name, factor in factors.items():
        out[name] = (out[name] * factor).astype(out[name].dtype)
    return out
```

```python
from contextlib import ExitStack

import numpy as np

import concourse.bass as bass
from concourse import mybir

F32 = mybir.dt.float32
U32 = mybir.dt.uint32
ALU = mybir.AluOpType
ACT = mybir.ActivationFunctionType
AX = mybir.AxisListType.X
ds = bass.ds

P = 128
D = 1024
KT = D // P
T = 1024 // P
B = 8
NC9 = B + 1
H = 8
HD = 64
HW = H * HD
G = H // 2
VA = HD + 1
SPAN = 2 * 1024 - P
NPROJ = 7
CHUNKS = NPROJ + 2
SEG = 2
WBUF = 3
ORDER = (4, 5, 0, 1, 2, 3, 6)
EPS = 1e-6
MASKED = -1e30
LOWEST = -3e38
HP = 8
TOPK = 16
NK = 128
SLOTS = HP * TOPK
RING = 8
GRP = 2
PAST = 1024
BRANCHES = ((128, 1), (512, 4), (2048, 16))
NSEL = 256
ADA_COLS = 512
ADA_CHUNKS = 6 * D // ADA_COLS


def halves(keys):
    return [slice(0, 512), slice(512, keys)] if keys > 512 else [slice(0, keys)]


def build(nc, a):
    with ExitStack() as whole:
        def sem(name):
            return whole.enter_context(nc.semaphore(name))

        ps = [whole.enter_context(nc.psum_tensor(f"bank{i}", [P, 512], F32)) for i in range(2)]
        psS = [whole.enter_context(nc.psum_tensor(f"pair{i}", [P, 1024], F32)) for i in range(2)]
        psO = [whole.enter_context(nc.psum_tensor(f"bank{6 + i}", [P, 512], F32)) for i in range(2)]

        def keep(name, shape, dt=F32):
            return whole.enter_context(nc.sbuf_tensor("sb_" + name, shape, dt))

        ident = keep("ident", [P, P])
        mod = keep("mod", [P, 48, NC9])
        gt2row = keep("gt2row", [P, D])
        tabs = keep("tabs", [P, 6, KT, NC9])
        front(nc, a, sem, ps, psS, psO, ident, mod, gt2row, tabs)
        decode(nc, a, sem, ps, psS, psO, ident, tabs)
        peer(nc, a, sem, ps, psS, psO, ident, gt2row)


def front(nc, a, sem, ps, psS, psO, ident, mod, gt2row, tabs):
    with ExitStack() as ctx:
        def sb(name, shape, dt=F32):
            return ctx.enter_context(nc.sbuf_tensor("sb_" + name, shape, dt))

        w = [sb(f"w{i}", [P, KT, 512]) for i in range(WBUF)]
        dist = sb("dist", [P, SPAN])
        count = sb("count", [P, SPAN])
        dist_t = sb("dist_t", [P, 1024])
        count_t = sb("count_t", [P, 1024])
        intra = sb("intra", [P, H * P])
        wstart = sb("wstart", [P, G * P])
        wend = sb("wend", [P, H])
        cdecay = sb("cdecay", [P, G])
        qkscale = sb("qkscale", [P, 2 * H])
        grow = sb("grow", [P, 2 * HW])
        gret = sb("gret", [P, HW])
        badaT = sb("badaT", [P, 48])
        gnT = sb("gnT", [P, 2, KT])
        cT = sb("cT", [P, KT, NC9])
        ones = sb("ones", [P, P])
        gt1row = sb("gt1row", [P, D])
        a2row = sb("a2row", [P, D])
        b2row = sb("b2row", [P, D])
        kT = sb("kT", [P, G, 1024])
        va = sb("va", [P, T, H * VA])
        xt = sb("xt", [P, D])
        xn = sb("xn", [P, D])
        hT = sb("hT", [P, KT, P])
        qk = sb("qk", [P, 2 * HW])
        qkn = sb("qkn", [P, 2 * HW])
        rq, rk, rv, srg, av = (sb(n, [P, HW]) for n in ("rq", "rk", "rv", "srg", "av"))
        turned = sb("turned", [P, 4, G, P])
        rqT, rkT, aqT, qTw = (turned[:, i] for i in range(4))
        kw = sb("kw", [P, HW])
        sT = sb("sT", [P, H * P])
        state = sb("state", [P, G, P])
        osb = sb("osb", [P, HW])
        sp = [sb(f"sp{i}", [P, 1024]) for i in range(2)]
        pt = [sb(f"pt{i}", [P, 1024]) for i in range(2)]
        mix = sb("mix", [P, D])
        arow, diagonals = (rq, rk), (*sp, *pt)
        mixT = turned[:, 0:2].rearrange("p a g i -> p (a g) i")
        xm, h2, junk, xres = qk, sp[0], xn, mix
        st = sb("st", [P, 64])
        ss, var, std, rstd = (st[:, i:i + 1] for i in range(4))
        nmax = st[:, 8:16]
        rden = st[:, 16:24]
        st16 = sb("st16", [P, 4, 16])
        ssq, varq, stdq, rstdq = (st16[:, i, :] for i in range(4))
        mu = sb("mu", [P, H])

        s_c = sem("conditioning_loaded")
        s_ident = sem("identity_loaded")
        s_const = sem("const_loaded")
        s_arow = sem("ada_rows_copied")
        s_adaT = sem("ada_rows_turned")
        s_tabs = sem("ada_tables")
        s_ada = [sem(f"ada_chunk{i}") for i in range(WBUF)]
        s_w = [sem(f"weight_chunk{i}") for i in range(WBUF)]
        s_silu = sem("silu_c")
        s_adamm = sem("ada_product")
        s_diag = sem("ada_diagonal")
        s_bc = sem("ada_broadcast")
        s_row = sem("ada_rows")
        s_init = sem("front_buffers_set")
        s_x = sem("x_loaded")
        s_xres = sem("residual_loaded")
        s_var = sem("variance")
        s_std = sem("deviation")
        s_xn = sem("x_normed")
        s_xT = sem("x_transposed")
        s_hT = sem("h_transposed")
        s_proj = sem("projected")
        s_evA = sem("projection_read_act")
        s_evD = sem("projection_read_dve")
        s_tr = sem("rows_transposed")
        s_te = sem("transposed_copied")
        s_qkn = sem("qk_normed")
        s_vaug = sem("values_placed")
        s_qTw = sem("q_decayed")
        s_kw = sem("k_decayed")
        s_rs = sem("ret_scores")
        s_sT = sem("ret_scores_decayed")
        s_oret = sem("ret_output")
        s_oread = sem("ret_output_read")
        s_state = sem("ret_state")
        s_S = sem("att_scores")
        s_nm = sem("att_max")
        s_P = sem("att_probs")
        s_pt = sem("att_probs_transposed")
        s_PT = sem("att_probs_weighted")
        s_pv = sem("att_output")
        s_mix = sem("mixed")
        s_mT = sem("mix_transposed")
        s_mixT = sem("mix_transposed_copied")
        s_wo = sem("out_projected")
        s_xm = sem("x_mid_half")
        s_h2 = sem("h2_ready")
        s_chain = sem("dve_step")
        s_passed = sem("front_wait_passed")
        s_owk = sem("stored_wk")
        s_owv = sem("stored_wv")
        s_oxm = sem("stored_x_mid")
        s_oh2 = sem("stored_h2")
        s_stored = sem("tiles_stored")
        s_oret_out = sem("stored_state")

        consts = [(dist, "c_dist"), (count, "c_count"), (intra, "c_intra"),
                  (wstart, "c_wstart"), (wend, "c_wend"), (cdecay, "c_cdecay"), (qkscale, "c_qkscale"),
                  (grow, "g_qk"), (gret, "g_ret_rows"), (badaT, "b_adaT"), (gnT, "gnT")]
        w_ada = a["w_ada"].rearrange("(k p) n -> p k n", p=P)
        w_in = a["w_in"].rearrange("(k p) n -> p k n", p=P)
        w_out = a["w_out"].rearrange("(k p) n -> p k n", p=P)
        nbuf = CHUNKS // WBUF
        assert CHUNKS % WBUF == 0 and ADA_CHUNKS % WBUF == 0

        block = ctx.enter_context(nc.Block())

        @block.sync
        def _(sp_):
            for begun in (s_wo, s_evA):
                sp_.sem_inc(begun, 1)
            sp_.dma_start(cT[:], a["cT"]).then_inc(s_c, 16)
            sp_.dma_start(ident[:], a["c_ident"]).then_inc(s_ident, 16)
            for c in range(ADA_CHUNKS):
                if c >= WBUF:
                    sp_.wait_ge(s_adamm, c - WBUF + 1)
                sp_.dma_start(w[c % WBUF][:], w_ada[:, :, c * 512:(c + 1) * 512]).then_inc(s_ada[c % WBUF], 16)
                if c == 2:
                    for tile, name in consts:
                        sp_.dma_start(tile[:], a[name]).then_inc(s_const, 16)
                    sp_.dma_start(xt[:], a["x_all"][0:P, :]).then_inc(s_x, 16)
            sp_.wait_ge(s_adamm, ADA_CHUNKS)
            with sp_.Fori(0, T) as t:
                for c in range(CHUNKS):
                    if 1 <= c < WBUF:
                        sp_.wait_ge(s_wo, t * 2 + 1)
                    elif c >= WBUF:
                        sp_.wait_ge(s_proj, t * NPROJ + c - WBUF + 1)
                    else:
                        sp_.wait_ge(s_evA, t * 5 + 1)
                    src = (w_in[:, :, ORDER[c] * HW:(ORDER[c] + 1) * HW] if c < NPROJ
                           else w_out[:, :, (c - NPROJ) * 512:(c - NPROJ + 1) * 512])
                    sp_.dma_start(w[c % WBUF][:], src).then_inc(s_w[c % WBUF], 16)
                    if c == WBUF:
                        sp_.wait_ge(s_xn, t + 1)
                        sp_.dma_start(xt[:], a["x_all"][ds((t + 1) * P, P), :]).then_inc(s_x, 16)
                sp_.wait_ge(s_mT, t * 2 + 2)
                sp_.dma_start(xres[:], a["x_all"][ds(t * P, P), :]).then_inc(s_xres, 16)

        @block.gpsimd
        def _(pool):
            pool.sem_inc(s_stored, 1)
            pool.memset(ones[:], 1.0).then_inc(s_init, 1)
            pool.memset(kT[:], 0.0).then_inc(s_init, 1)
            pool.memset(va[:], 1.0).then_inc(s_init, 1)
            pool.memset(state[:], 0.0).then_inc(s_init, 1)
            with pool.Fori(0, T) as t:
                row = ds(t * P, P)
                pool.wait_ge(s_qkn, t + 1)
                pool.sem_inc(s_passed, 1)
                pool.dma_start(a["wk_prompt"][row, :], qkn[:, HW:2 * HW]).then_inc(s_owk, 16)
                pool.wait_ge(s_evA, t * 5 + 6)
                pool.sem_inc(s_passed, 1)
                pool.dma_start(a["wv_prompt"][row, :], av[:]).then_inc(s_owv, 16)
                pool.wait_ge(s_h2, t + 1)
                pool.sem_inc(s_passed, 1)
                pool.dma_start(a["x_mid"][row, :], xm[:]).then_inc(s_oxm, 16)
                pool.dma_start(a["h2"][row, :], h2[:]).then_inc(s_oh2, 16)
                for out in (s_owk, s_owv, s_oxm, s_oh2):
                    pool.wait_ge(out, t * 16 + 16)
                pool.sem_inc(s_stored, 1)
            pool.wait_ge(s_state, 2 * T + 1)
            ret = a["ret_prompt"].rearrange("(g e d) f -> e d g f", e=2, d=HD)
            for e in range(2):
                pool.dma_start(ret[e], state[e * HD:(e + 1) * HD, :, e * HD:(e + 1) * HD]).then_inc(s_oret_out, 16)
            pool.wait_ge(s_oret_out, 32)

        @block.scalar
        def _(act):
            act.wait_ge(s_c, 16)
            act.activation(cT[:], cT[:], ACT.Silu).then_inc(s_silu, 1)
            for c in range(ADA_CHUNKS):
                act.wait_ge(s_adamm, c + 1)
                if c >= 2:
                    act.wait_ge(s_adaT, c - 1)
                act.activation(arow[c % 2][0:NC9, :], ps[c % 2][0:NC9, :], ACT.Copy).then_inc(s_arow, 1)

            def x_turned(n):
                for half in range(2):
                    act.wait_ge(s_xT, n * 2 + half + 1)
                    for j in range(4):
                        k = half * 4 + j
                        last = act.activation(hT[:, k, :], psS[1][:, k * P:(k + 1) * P], ACT.Identity,
                                              scale=tabs[:, 0, k, B:B + 1], bias=tabs[:, 1, k, B:B + 1])
                    last.then_inc(s_hT, 1)

            act.wait_ge(s_var, 1)
            act.activation(std, var, ACT.Sqrt).then_inc(s_std, 1)
            act.wait_ge(s_tabs, 1)
            x_turned(0)
            for n, row in enumerate((gt1row, a2row, b2row, gt2row)):
                act.wait_ge(s_bc, n + 1)
                act.activation(row[:], psS[n % 2][:], ACT.Copy).then_inc(s_row, 1)
            for first in range(0, T, SEG):
                keys = (first + SEG) * P
                with act.Fori(first, first + SEG) as t:
                    def read(n, dst, src, func=ACT.Copy):
                        act.wait_ge(s_proj, t * NPROJ + n)
                        act.activation(dst[:], src, func).then_inc(s_evA, 1)

                    def copy_turned(n, out):
                        act.wait_ge(s_tr, t * 4 + n + 1)
                        act.activation(out, ps[n % 2][:].rearrange("p (g i) -> p g i", g=G), ACT.Copy).then_inc(s_te, 1)

                    read(3, rq, psS[0][:, 0:512])
                    read(4, rk, psS[0][:, 512:1024])
                    act.wait_ge(s_var, t * 4 + 2)
                    act.activation(stdq, varq, ACT.Sqrt).then_inc(s_std, 1)
                    read(5, rv, psS[1][:, 0:512])
                    copy_turned(0, rqT)
                    read(6, srg, psS[1][:, 512:1024], ACT.Silu)
                    copy_turned(1, rkT)
                    act.wait_ge(s_stored, t + 1)
                    read(7, av, psS[0][:, 0:512])
                    copy_turned(2, aqT)
                    copy_turned(3, kT[:, :, ds(t * P, P)])
                    for h in range(H):
                        act.wait_ge(s_nm, t * H + h + 1)
                        act.activation(sp[h % 2][:, 0:keys], sp[h % 2][:, 0:keys], ACT.Exp,
                                       bias=nmax[:, h:h + 1]).then_inc(s_P, 1)
                        if h == 2:
                            act.wait_ge(s_var, t * 4 + 3)
                            act.activation(stdq[:, 0:H], varq[:, 0:H], ACT.Sqrt).then_inc(s_std, 1)
                        if h == H - 2:
                            act.wait_ge(s_var, t * 4 + 4)
                            act.activation(std, var, ACT.Sqrt).then_inc(s_std, 1)
                    x_turned(t + 1)
                    for half in range(2):
                        act.wait_ge(s_mT, t * 2 + half + 1)
                        act.activation(mixT[:, half * 4:half * 4 + 4, :],
                                       ps[half][:].rearrange("p (g i) -> p g i", g=4), ACT.Copy).then_inc(s_mixT, 1)
                    act.wait_ge(s_var, t * 4 + 5)
                    act.activation(std, var, ACT.Sqrt).then_inc(s_std, 1)

        @block.vector
        def _(dve):
            steps = [0]

            def step(ins):
                steps[0] += 1
                ins.then_inc(s_chain, 1)
                dve.wait_ge(s_chain, steps[0])

            def restart():
                dve.sem_clear(s_chain)
                steps[0] = 0

            def x_variance(n):
                dve.wait_ge(s_x, n * 16 + 16)
                step(dve.tensor_tensor_reduce(junk[:], xt[:], xt[:], 1.0, 0.0, ALU.mult, ALU.add, ss))
                dve.tensor_scalar(var, ss, 1.0 / D, EPS, ALU.mult, ALU.add).then_inc(s_var, 1)

            def x_scale(count):
                dve.wait_ge(s_std, count)
                step(dve.reciprocal(rstd, std))
                dve.tensor_scalar(xn[:], xt[:], rstd, None, ALU.mult).then_inc(s_xn, 1)

            x_variance(0)
            x_scale(1)

            dve.wait_ge(s_adaT, ADA_CHUNKS)
            dve.wait_ge(s_const, 16 * len(consts))
            step(dve.tensor_tensor(mod[:], psO[1][:, 0:48 * NC9].rearrange("p (m c) -> p m c", c=NC9),
                                   badaT[:].unsqueeze(2).to_broadcast([P, 48, NC9]), ALU.add))
            sec = [mod[:, s * KT:(s + 1) * KT, :] for s in range(6)]
            for n, (sc, sh, gt) in enumerate(((1, 0, 2), (4, 3, 5))):
                gb = gnT[:, n, :].unsqueeze(2).to_broadcast([P, KT, NC9])
                step(dve.scalar_tensor_tensor(out=tabs[:, 3 * n, :, :], in0=sec[sc], scalar=1.0, in1=gb,
                                              op0=ALU.add, op1=ALU.mult))
                step(dve.tensor_copy(tabs[:, 3 * n + 1, :, :], sec[sh]))
                dve.tensor_copy(tabs[:, 3 * n + 2, :, :], sec[gt]).then_inc(s_tabs, 1)
            dve.wait_ge(s_tabs, 2)
            for n, sec_no in enumerate((2, 3, 4, 5)):
                dve.tensor_tensor(diagonals[n][:].rearrange("p (k i) -> p k i", k=KT),
                                  ident[:].unsqueeze(1).to_broadcast([P, KT, P]),
                                  tabs[:, sec_no, :, B:B + 1].to_broadcast([P, KT, P]), ALU.mult).then_inc(s_diag, 1)
            dve.wait_ge(s_init, 4)
            dve.wait_ge(s_row, 4)

            for first in range(0, T, SEG):
                keys = (first + SEG) * P
                with dve.Fori(first, first + SEG) as t:
                    restart()
                    off = (T - 1) * P - t * P
                    step(dve.tensor_copy(dist_t[:, 0:keys], dist[:, ds(off, keys)]))
                    step(dve.tensor_copy(count_t[:, 0:keys], count[:, ds(off, keys)]))
                    dve.wait_ge(s_stored, t + 1)
                    for n in range(2):
                        dve.wait_ge(s_proj, t * NPROJ + n + 1)
                        dve.tensor_copy(qk[:, n * HW:(n + 1) * HW], psS[1][:, n * 512:(n + 1) * 512]).then_inc(s_evD, 1)
                    dve.wait_ge(s_evD, t * 2 + 2)
                    step(dve.tensor_tensor(junk[:], qk[:], qk[:], ALU.mult))
                    step(dve.tensor_reduce(ssq, junk[:].rearrange("p (h d) -> p h d", d=HD), AX, ALU.add))
                    dve.tensor_scalar(varq, ssq, 1.0 / HD, EPS, ALU.mult, ALU.add).then_inc(s_var, 1)
                    dve.wait_ge(s_std, t * 4 + 2)
                    step(dve.reciprocal(rstdq, stdq))
                    step(dve.tensor_tensor(rstdq, rstdq, qkscale[:], ALU.mult))
                    step(dve.tensor_tensor(qk[:].rearrange("p (h d) -> p h d", d=HD),
                                           qk[:].rearrange("p (h d) -> p h d", d=HD),
                                           rstdq.unsqueeze(2).to_broadcast([P, 2 * H, HD]), ALU.mult))
                    dve.tensor_tensor(qkn[:], qk[:], grow[:], ALU.mult).then_inc(s_qkn, 1)
                    dve.wait_ge(s_evA, t * 5 + 3)
                    dve.tensor_tensor(kw[:].rearrange("p (h d) -> p h d", d=HD), rk[:].rearrange("p (h d) -> p h d", d=HD),
                                      wend[:].unsqueeze(2).to_broadcast([P, H, HD]), ALU.mult).then_inc(s_kw, 1)
                    dve.wait_ge(s_te, t * 4 + 1)
                    dve.tensor_tensor(qTw[:], rqT[:], wstart[:].rearrange("p (g i) -> p g i", g=G), ALU.mult)\
                       .then_inc(s_qTw, 1)
                    dve.wait_ge(s_evA, t * 5 + 6)
                    dve.tensor_copy(va[:, ds(t, 1), :].rearrange("p o (h e) -> p (o h) e", e=VA)[:, :, 0:HD],
                                    av[:].rearrange("p (h d) -> p h d", d=HD)).then_inc(s_vaug, 1)
                    for half in range(2):
                        dve.wait_ge(s_rs, t * 2 + half + 1)
                        c = slice(half * 512, half * 512 + 512)
                        dve.tensor_tensor(sT[:, c], psS[1][:, c], intra[:, c], ALU.mult).then_inc(s_sT, 1)
                    def att_max(h):
                        dve.wait_ge(s_S, t * H + h + 1)
                        if h >= 2:
                            dve.wait_ge(s_pt, t * 2 * H + 2 * (h - 2) + 2)
                        dve.sem_inc(s_passed, 1)
                        step(dve.tensor_tensor_reduce(sp[h % 2][:, 0:keys], psS[h % 2][:, 0:keys], dist_t[:, 0:keys],
                                                      2.0 ** -(h + 1), LOWEST,
                                                      ALU.add, ALU.max, nmax[:, h:h + 1]))
                        dve.tensor_scalar(nmax[:, h:h + 1], nmax[:, h:h + 1], -1.0, None, ALU.mult).then_inc(s_nm, 1)

                    def att_weigh(h):
                        if h >= 2:
                            dve.wait_ge(s_pv, t * H + h - 1)
                        for half, c in enumerate(halves(keys)):
                            dve.wait_ge(s_pt, t * 2 * H + 2 * h + half + 1)
                            dve.tensor_tensor(pt[h % 2][:, c], ps[half][:, 0:c.stop - c.start], count_t[:, c],
                                              ALU.mult).then_inc(s_PT, 2 // len(halves(keys)))

                    def groupnorm():
                        o3 = osb[:].rearrange("p (h d) -> p h d", d=HD)
                        j3 = junk[:, 0:HW].rearrange("p (h d) -> p h d", d=HD)
                        dve.wait_ge(s_oread, t + 1)
                        step(dve.tensor_reduce(mu[:], o3, AX, ALU.add))
                        step(dve.tensor_scalar(mu[:], mu[:], -1.0 / HD, None, ALU.mult))
                        step(dve.tensor_tensor(o3, o3, mu[:].unsqueeze(2).to_broadcast([P, H, HD]), ALU.add))
                        step(dve.tensor_tensor(j3, o3, o3, ALU.mult))
                        step(dve.tensor_reduce(ssq[:, 0:H], j3, AX, ALU.add))
                        dve.tensor_scalar(varq[:, 0:H], ssq[:, 0:H], 1.0 / HD, EPS, ALU.mult, ALU.add).then_inc(s_var, 1)

                    def gate():
                        o3 = osb[:].rearrange("p (h d) -> p h d", d=HD)
                        dve.wait_ge(s_std, t * 4 + 3)
                        step(dve.reciprocal(rstdq[:, 0:H], stdq[:, 0:H]))
                        step(dve.tensor_tensor(o3, o3, rstdq[:, 0:H].unsqueeze(2).to_broadcast([P, H, HD]), ALU.mult))
                        step(dve.tensor_tensor(osb[:], osb[:], gret[:], ALU.mult))
                        step(dve.tensor_tensor(mix[:].rearrange("p (h c) -> p h c", h=H)[:, :, 0:HD], o3,
                                               srg[:].rearrange("p (h d) -> p h d", d=HD), ALU.mult))

                    att_max(0)
                    dve.wait_ge(s_oret, t + 1)
                    dve.tensor_copy(osb[:], psO[0][:, 0:HW]).then_inc(s_oread, 1)
                    kv = psO[1][:].rearrange("p (g c) -> p g c", c=P)
                    for par in range(2):
                        e = slice(par * HD, par * HD + HD)
                        step(dve.tensor_tensor(state[e, :, e], state[e, :, e],
                                               cdecay[e, :].unsqueeze(2).to_broadcast([HD, G, HD]), ALU.mult))
                        dve.tensor_tensor(state[e, :, e], state[e, :, e], kv[e, :, e], ALU.add).then_inc(s_state, 1)
                    att_max(1)
                    for h in range(H):
                        att_weigh(h)
                        if h + 2 < H:
                            att_max(h + 2)
                        if h == 0:
                            groupnorm()
                        if h == 2:
                            gate()
                        if h == H - 4:
                            x_variance(t + 1)
                        if h == H - 3:
                            x_scale(t * 4 + 4)
                    dve.wait_ge(s_pv, t * H + H)
                    for n in range(2):
                        o = psO[n][:, 0:4 * VA].rearrange("p (h e) -> p h e", e=VA)
                        rd = rden[:, 4 * n:4 * n + 4]
                        step(dve.reciprocal(rd.unsqueeze(2), o[:, :, HD:VA]))
                        dve.tensor_tensor(mix[:].rearrange("p (h c) -> p h c", h=H)[:, 4 * n:4 * n + 4, HD:2 * HD],
                                          o[:, :, 0:HD], rd.unsqueeze(2).to_broadcast([P, 4, HD]), ALU.mult)\
                           .then_inc(s_mix, 1)
                    dve.wait_ge(s_xres, t * 16 + 16)
                    for half in range(2):
                        c = slice(half * 512, half * 512 + 512)
                        dve.wait_ge(s_wo, t * 2 + half + 2)
                        step(dve.tensor_tensor(xm[:, c], psS[0][:, c], gt1row[:, c], ALU.mult))
                        dve.tensor_tensor(xm[:, c], xm[:, c], xres[:, c], ALU.add).then_inc(s_xm, 1)
                    dve.wait_ge(s_xm, t * 2 + 3)
                    step(dve.tensor_tensor_reduce(junk[:], xm[:], xm[:], 1.0, 0.0, ALU.mult, ALU.add, ss))
                    dve.tensor_scalar(var, ss, 1.0 / D, EPS, ALU.mult, ALU.add).then_inc(s_var, 1)
                    dve.wait_ge(s_std, t * 4 + 5)
                    step(dve.reciprocal(rstd, std))
                    step(dve.scalar_tensor_tensor(out=h2[:], in0=xm[:], scalar=rstd, in1=a2row[:],
                                                  op0=ALU.mult, op1=ALU.mult))
                    dve.tensor_tensor(h2[:], h2[:], b2row[:], ALU.add).then_inc(s_h2, 1)

        @block.tensor
        def _(pe):
            for begun in (s_xm, s_state):
                pe.sem_inc(begun, 1)
            def turn_ada(c):
                pe.wait_ge(s_arow, c + 1)
                for m in range(4):
                    col = (c * 4 + m) * NC9
                    last = pe.transpose(psO[1][:, col:col + NC9], arow[c % 2][0:NC9, m * P:(m + 1) * P],
                                        ident[0:NC9, 0:NC9])
                last.then_inc(s_adaT, 1)

            pe.wait_ge(s_silu, 1)
            pe.wait_ge(s_ident, 16)
            for c in range(ADA_CHUNKS):
                pe.wait_ge(s_ada[c % WBUF], 16 * (c // WBUF + 1))
                if c >= 2:
                    pe.wait_ge(s_arow, c - 1)
                for k in range(KT):
                    last = pe.matmul(ps[c % 2][0:NC9, :], cT[:, k, :], w[c % WBUF][:, k, :],
                                     start=(k == 0), stop=(k == KT - 1))
                last.then_inc(s_adamm, 1)
                if c >= 1:
                    turn_ada(c - 1)
            turn_ada(ADA_CHUNKS - 1)

            def turn_x(n):
                pe.wait_ge(s_xn, n + 1)
                for half in range(2):
                    for j in range(4):
                        k = half * 4 + j
                        last = pe.transpose(psS[1][:, k * P:(k + 1) * P], xn[:, k * P:(k + 1) * P], ident[:])
                    last.then_inc(s_xT, 1)

            turn_x(0)
            pe.wait_ge(s_init, 4)
            for n in range(4):
                pe.wait_ge(s_diag, n + 1)
                if n == 1:
                    pe.wait_ge(s_hT, 2)
                if n >= 2:
                    pe.wait_ge(s_row, n - 1)
                for half in range(2):
                    c = slice(half * 512, half * 512 + 512)
                    last = pe.matmul(psS[n % 2][:, c], ones[:], diagonals[n][:, c], start=True, stop=True)
                last.then_inc(s_bc, 1)
            pe.wait_ge(s_row, 4)
            for first in range(0, T, SEG):
                keys = (first + SEG) * P
                with pe.Fori(first, first + SEG) as t:
                    def turn(src, n):
                        if n >= 2:
                            pe.wait_ge(s_te, t * 4 + n - 1)
                        for g in range(G):
                            last = pe.transpose(ps[n % 2][:, g * P:(g + 1) * P], src[:, g * P:(g + 1) * P], ident[:])
                        last.then_inc(s_tr, 1)

                    pe.wait_ge(s_hT, t * 2 + 2)
                    for c in range(NPROJ):
                        pe.wait_ge(s_w[c % WBUF], t * 16 * nbuf + 16 * (c // WBUF + 1))
                        if c == 2:
                            pe.wait_ge(s_xm, t * 2 + 1)
                        if c == 4:
                            pe.wait_ge(s_evD, t * 2 + 1)
                        if c == 5:
                            pe.wait_ge(s_evD, t * 2 + 2)
                        if c == 6:
                            pe.wait_ge(s_evA, t * 5 + 2)
                        bank = psS[1 - (c // 2) % 2][:, (c % 2) * 512:(c % 2) * 512 + 512]
                        for k in range(KT):
                            last = pe.matmul(bank, hT[:, k, :], w[c % WBUF][:, k, :], start=(k == 0), stop=(k == KT - 1))
                        last.then_inc(s_proj, 1)
                        if c == 4:
                            pe.wait_ge(s_evA, t * 5 + 2)
                            turn(rq, 0)
                        if c == 5:
                            pe.wait_ge(s_evA, t * 5 + 3)
                            turn(rk, 1)
                    pe.wait_ge(s_qkn, t + 1)
                    turn(qkn, 2)
                    turn(qkn[:, HW:2 * HW], 3)
                    pe.wait_ge(s_te, t * 4 + 2)
                    pe.wait_ge(s_evA, t * 5 + 5)
                    for par in range(2):
                        e = slice(par * HD, par * HD + HD)
                        for g in range(G):
                            c = (par * G + g) * P
                            last = pe.matmul(psS[1][:, c:c + P], rkT[e, g, :], rqT[e, g, :], start=True, stop=True)
                        last.then_inc(s_rs, 1)
                    pe.wait_ge(s_kw, t + 1)
                    pe.wait_ge(s_state, t * 2 + 1)
                    for g in range(G):
                        c = slice(g * P, g * P + P)
                        pe.matmul(psO[1][:, c], kw[:, c], rv[:, c], start=True, stop=True)
                    def scores(h):
                        e = slice((h % 2) * HD, (h % 2) * HD + HD)
                        if h >= 2:
                            pe.wait_ge(s_nm, t * H + h - 1)
                        for c in halves(keys):
                            last = pe.matmul(psS[h % 2][:, c], aqT[e, h // 2, :], kT[e, h // 2, c], start=True, stop=True)
                        last.then_inc(s_S, 1)

                    pe.wait_ge(s_te, t * 4 + 4)
                    pe.wait_ge(s_evA, t * 5 + 6)
                    scores(0)
                    pe.wait_ge(s_qTw, t + 1)
                    pe.wait_ge(s_sT, t * 2 + 2)
                    for g in range(G):
                        pe.matmul(psO[0][:, g * P:(g + 1) * P], qTw[:, g, :], state[:, g, :], start=True, stop=False)
                        for par in range(2):
                            c, o = (par * G + g) * P, (2 * g + par) * HD
                            last = pe.matmul(psO[0][:, o:o + HD], sT[:, c:c + P], rv[:, o:o + HD],
                                             start=False, stop=(par == 1))
                    last.then_inc(s_oret, 1)

                    scores(1)
                    for h in range(H):
                        pe.wait_ge(s_P, t * H + h + 1)
                        for half, c in enumerate(halves(keys)):
                            if h >= 1:
                                pe.wait_ge(s_PT, t * 2 * H + 2 * (h - 1) + half + 1)
                            for k in range(c.start // P, c.stop // P):
                                j = k - half * 4
                                last = pe.transpose(ps[half][:, j * P:(j + 1) * P],
                                                    sp[h % 2][:, k * P:(k + 1) * P], ident[:])
                            last.then_inc(s_pt, 2 // len(halves(keys)))
                        if h + 2 < H:
                            scores(h + 2)
                        if h == H - 1:
                            turn_x(t + 1)
                        if h == 0:
                            pe.wait_ge(s_vaug, t + 1)
                            pe.wait_ge(s_oread, t + 1)
                            pe.wait_ge(s_state, t * 2 + 3)
                        pe.wait_ge(s_PT, t * 2 * H + 2 * h + 2)
                        for k in range(keys // P):
                            last = pe.matmul(psO[h // 4][:, (h % 4) * VA:(h % 4) * VA + VA], pt[h % 2][:, k * P:(k + 1) * P],
                                             va[:, k, h * VA:(h + 1) * VA], start=(k == 0), stop=(k == keys // P - 1))
                        last.then_inc(s_pv, 1)
                    pe.wait_ge(s_mix, t * 2 + 2)
                    for half in range(2):
                        for j in range(4):
                            k = half * 4 + j
                            last = pe.transpose(ps[half][:, j * P:(j + 1) * P], mix[:, k * P:(k + 1) * P], ident[:])
                        last.then_inc(s_mT, 1)
                    pe.wait_ge(s_mixT, t * 2 + 2)
                    for c in range(NPROJ, CHUNKS):
                        pe.wait_ge(s_w[c % WBUF], t * 16 * nbuf + 16 * (c // WBUF + 1))
                        n = c - NPROJ
                        for k in range(KT):
                            last = pe.matmul(psS[0][:, n * 512:(n + 1) * 512], mixT[:, k, :], w[c % WBUF][:, k, :],
                                             start=(k == 0), stop=(k == KT - 1))
                        last.then_inc(s_wo, 1)


def decode(nc, a, sem, ps, psS, psO, ident, tabs):
    BH = B * H
    LOTS = 4
    with ExitStack() as ctx:
        def sb(name, shape, dt=F32):
            return ctx.enter_context(nc.sbuf_tensor("de_" + name, shape, dt))

        w = [sb(f"w{i}", [P, KT, 512]) for i in range(WBUF)]
        xs = sb("xs", [B, D])
        xns = sb("xns", [B, D])
        junk = sb("junk", [B, D])
        xms = sb("xms", [B, D])
        h2s = sb("h2s", [B, D])
        rows = sb("rows", [B, 4, D])
        hTs = sb("hTs", [P, KT, B])
        mixs = sb("mixs", [B, D])
        mixTs = sb("mixTs", [P, KT, B])
        proj = sb("proj", [B, NPROJ, HW])
        pj = sb("pj", [BH, NPROJ, HD])
        gqk = sb("gqk", [BH, 2, HD])
        gret = sb("gret", [BH, HD])
        gamma = sb("gamma", [BH, 1])
        bias = sb("bias", [BH, NSEL + 1])
        count = sb("count", [BH, NSEL + 1])
        s0 = sb("s0", [BH, HD, HD])
        prod = sb("prod", [BH, HD, HD])
        kv = [sb(f"kv{i}", [BH, HD * HD]) for i in range(2)]
        sq = sb("sq", [BH, 2, HD])
        o = sb("o", [BH, HD])
        osum = sb("osum", [BH, HD])
        part = sb("part", [BH, HD])
        srg = sb("srg", [BH, HD])
        mix = sb("mix", [BH, 2, HD])
        S = sb("S", [BH, NSEL + 1])
        st = sb("st", [BH, 16])
        stB = sb("stB", [B, 4])
        zeros = sb("zeros", [P, D])

        s_ld = sem("sample_loaded")
        s_w = [sem(f"sample_weight{i}") for i in range(WBUF)]
        s_kv = [sem(f"sample_cache{i}") for i in range(2)]
        s_kvu = sem("sample_cache_used")
        s_var = sem("sample_variance")
        s_std = sem("sample_deviation")
        s_xn = sem("sample_normed")
        s_tr = sem("sample_turned_psum")
        s_hT = sem("sample_turned_copied")
        s_rows = sem("sample_rows_psum")
        s_rowc = sem("sample_rows_copied")
        s_proj = sem("sample_projected")
        s_pc = sem("sample_projection_copied")
        s_pst = sem("sample_projection_stored")
        s_pj = sem("sample_heads_loaded")
        s_akn = sem("sample_keys_normed")
        s_silu = sem("sample_silu")
        s_state = sem("sample_state")
        s_max = sem("sample_max")
        s_exp = sem("sample_exp")
        s_mix = sem("sample_mixed")
        s_mst = sem("sample_mix_stored")
        s_mld = sem("sample_mix_loaded")
        s_mT = sem("sample_mix_turned")
        s_mTc = sem("sample_mix_turned_copied")
        s_wo = sem("sample_out_projected")
        s_h2 = sem("sample_h2")
        s_z = sem("sample_zeros")
        s_st = sem("sample_stored")
        s_ch = sem("sample_dve_step")

        w_in = a["w_in"].rearrange("(k p) n -> p k n", p=P)
        w_out = a["w_out"].rearrange("(k p) n -> p k n", p=P)
        smalls = [(xs, "x_sample"), (gqk, "g_qk_s"), (gret, "g_ret_s"), (gamma, "c_gamma"), (bias, "c_bias_s"),
                  (count, "c_count_s"), (s0, "state_s")]
        STORES = 6
        block = ctx.enter_context(nc.Block())

        @block.sync
        def _(sp):
            for tile, name in smalls:
                sp.dma_start(tile[:], a[name]).then_inc(s_ld, 16)
            for c in range(CHUNKS):
                if c >= WBUF:
                    sp.wait_ge(s_proj, c - WBUF + 1)
                src = (w_in[:, :, c * HW:(c + 1) * HW] if c < NPROJ
                       else w_out[:, :, (c - NPROJ) * 512:(c - NPROJ + 1) * 512])
                sp.dma_start(w[c % WBUF][:], src).then_inc(s_w[c % WBUF], 16)
            for n in range(2 * LOTS):
                if n >= 2:
                    sp.wait_ge(s_kvu, n - 1)
                src = a["k_sel" if n < LOTS else "v_sel"][:, ds((n % LOTS) * HD * HD, HD * HD)]
                sp.dma_start(kv[n % 2][:], src).then_inc(s_kv[n % 2], 16)

        @block.gpsimd
        def _(pool):
            pool.memset(zeros[:], 0.0).then_inc(s_z, 1)
            pool.wait_ge(s_z, 1)
            pool.dma_start(a["h2"][T * P + B:(T + 1) * P, :], zeros[0:P - B, :]).then_inc(s_st, 16)
            pool.wait_ge(s_pc, NPROJ)
            pool.dma_start(a["proj_s"].rearrange("s b n -> b s n"), proj[:]).then_inc(s_pst, 16)
            pool.wait_ge(s_pst, 16)
            pool.dma_start(pj[:], a["proj_s"].rearrange("s b (h d) -> (b h) s d", d=HD)).then_inc(s_pj, 16)
            pool.wait_ge(s_pj, 16)
            pool.dma_start(a["wv_sample"], pj[:, 6, :]).then_inc(s_st, 16)
            pool.wait_ge(s_akn, 1)
            pool.dma_start(a["wk_sample"], pj[:, 5, :]).then_inc(s_st, 16)
            pool.wait_ge(s_state, 1)
            pool.dma_start(a["ret_sample"], s0[:].rearrange("p d e -> p (d e)")).then_inc(s_st, 16)
            pool.wait_ge(s_mix, 1)
            pool.dma_start(a["mix_s"], mix[:].rearrange("p c d -> p (c d)")).then_inc(s_mst, 16)
            pool.wait_ge(s_mst, 16)
            pool.dma_start(mixs[:], a["mix_s"].rearrange("(b h) c -> b (h c)", b=B)).then_inc(s_mld, 16)
            pool.wait_ge(s_rowc, 4)
            pool.dma_start(a["gt2_sample"], rows[:, 3, :]).then_inc(s_st, 16)
            pool.wait_ge(s_h2, 2)
            pool.dma_start(a["x_mid"][T * P:T * P + B, :], xms[:]).then_inc(s_st, 16)
            pool.dma_start(a["h2"][T * P:T * P + B, :], h2s[:]).then_inc(s_st, 16)
            pool.wait_ge(s_st, 16 * (STORES + 1))

        @block.scalar
        def _(act):
            for n in range(4):
                act.wait_ge(s_rows, n + 1)
                act.activation(rows[:, n, :], psS[n % 2][0:B, :], ACT.Copy).then_inc(s_rowc, 1)
            act.wait_ge(s_var, 1)
            act.activation(stB[:, 2:3], stB[:, 1:2], ACT.Sqrt).then_inc(s_std, 1)
            for c in range(NPROJ):
                act.wait_ge(s_proj, c + 1)
                act.activation(proj[:, c, :], ps[c % 2][0:B, :], ACT.Copy).then_inc(s_pc, 1)
            act.wait_ge(s_pj, 16)
            act.activation(srg[:], pj[:, 3, :], ACT.Silu).then_inc(s_silu, 1)
            act.wait_ge(s_var, 2)
            act.activation(st[:, 4:6], st[:, 2:4], ACT.Sqrt).then_inc(s_std, 1)
            act.wait_ge(s_var, 3)
            act.activation(st[:, 9:10], st[:, 8:9], ACT.Sqrt).then_inc(s_std, 1)
            act.wait_ge(s_max, 1)
            act.activation(S[:], S[:], ACT.Exp, bias=st[:, 11:12]).then_inc(s_exp, 1)
            act.wait_ge(s_var, 4)
            act.activation(stB[:, 2:3], stB[:, 1:2], ACT.Sqrt).then_inc(s_std, 1)

        @block.tensor
        def _(pe):
            for n, sec_no in enumerate((2, 3, 4, 5)):
                if n >= 2:
                    pe.wait_ge(s_rowc, n - 1)
                for k in range(KT):
                    last = pe.transpose(psS[n % 2][0:B, k * P:(k + 1) * P], tabs[:, sec_no, k, 0:B], ident[:])
                last.then_inc(s_rows, 1)
            pe.wait_ge(s_xn, 1)
            for k in range(KT):
                last = pe.transpose(psO[0][:, k * B:(k + 1) * B], xns[:, k * P:(k + 1) * P], ident[0:B, 0:B])
            last.then_inc(s_tr, 1)
            pe.wait_ge(s_hT, 1)
            for c in range(NPROJ):
                pe.wait_ge(s_w[c % WBUF], 16 * (c // WBUF + 1))
                if c >= 2:
                    pe.wait_ge(s_pc, c - 1)
                for k in range(KT):
                    last = pe.matmul(ps[c % 2][0:B, :], hTs[:, k, :], w[c % WBUF][:, k, :],
                                     start=(k == 0), stop=(k == KT - 1))
                last.then_inc(s_proj, 1)
            pe.wait_ge(s_mld, 16)
            for k in range(KT):
                last = pe.transpose(psO[1][:, k * B:(k + 1) * B], mixs[:, k * P:(k + 1) * P], ident[0:B, 0:B])
            last.then_inc(s_mT, 1)
            pe.wait_ge(s_mTc, 1)
            pe.wait_ge(s_rowc, 4)
            for c in range(NPROJ, CHUNKS):
                pe.wait_ge(s_w[c % WBUF], 16 * (c // WBUF + 1))
                n = c - NPROJ
                for k in range(KT):
                    last = pe.matmul(psS[0][0:B, n * 512:(n + 1) * 512], mixTs[:, k, :], w[c % WBUF][:, k, :],
                                     start=(k == 0), stop=(k == KT - 1))
                last.then_inc(s_wo, 1)

        @block.vector
        def _(dve):
            steps = [0]

            def step(ins):
                steps[0] += 1
                ins.then_inc(s_ch, 1)
                dve.wait_ge(s_ch, steps[0])

            def norm(src, n):
                step(dve.tensor_tensor_reduce(junk[:], src[:], src[:], 1.0, 0.0, ALU.mult, ALU.add, stB[:, 0:1]))
                dve.tensor_scalar(stB[:, 1:2], stB[:, 0:1], 1.0 / D, EPS, ALU.mult, ALU.add).then_inc(s_var, 1)
                dve.wait_ge(s_std, n)
                step(dve.reciprocal(stB[:, 3:4], stB[:, 2:3]))

            dve.wait_ge(s_ld, 16 * len(smalls))
            norm(xs, 1)
            dve.tensor_scalar(xns[:], xs[:], stB[:, 3:4], None, ALU.mult).then_inc(s_xn, 1)
            dve.wait_ge(s_tr, 1)
            step(dve.tensor_tensor(hTs[:], psO[0][:, 0:KT * B].rearrange("p (k b) -> p k b", b=B),
                                   tabs[:, 0, :, 0:B], ALU.mult))
            dve.tensor_tensor(hTs[:], hTs[:], tabs[:, 1, :, 0:B], ALU.add).then_inc(s_hT, 1)
            dve.wait_ge(s_pj, 16)
            qk = pj[:, 4:6, :]
            step(dve.tensor_tensor(sq[:], qk, qk, ALU.mult))
            step(dve.tensor_reduce(st[:, 0:2], sq[:], AX, ALU.add))
            dve.tensor_scalar(st[:, 2:4], st[:, 0:2], 1.0 / HD, EPS, ALU.mult, ALU.add).then_inc(s_var, 1)
            dve.wait_ge(s_std, 2)
            step(dve.reciprocal(st[:, 6:8], st[:, 4:6]))
            step(dve.tensor_tensor(qk, qk, st[:, 6:8].unsqueeze(2).to_broadcast([BH, 2, HD]), ALU.mult))
            dve.tensor_tensor(qk, qk, gqk[:], ALU.mult).then_inc(s_akn, 1)
            dve.wait_ge(s_akn, 1)
            rq, rk, rv, aq, ak, av = (pj[:, i, :] for i in (0, 1, 2, 4, 5, 6))
            step(dve.tensor_scalar(rk, rk, HD ** -0.5, None, ALU.mult))
            step(dve.tensor_scalar(aq, aq, HD ** -0.5, None, ALU.mult))
            step(dve.tensor_tensor(prod[:], s0[:], rq.unsqueeze(2).to_broadcast([BH, HD, HD]), ALU.mult))
            step(dve.tensor_reduce(o[:], prod[:].rearrange("p d e -> p e d"), AX, ALU.add))
            step(dve.tensor_tensor_reduce(sq[:, 0, :], rq, rk, 1.0, 0.0, ALU.mult, ALU.add, st[:, 12:13]))
            step(dve.tensor_scalar(sq[:, 1, :], rv, st[:, 12:13], None, ALU.mult))
            step(dve.scalar_tensor_tensor(out=o[:], in0=o[:], scalar=gamma[:], in1=sq[:, 1, :],
                                          op0=ALU.mult, op1=ALU.add))
            step(dve.tensor_tensor(prod[:], rk.unsqueeze(2).to_broadcast([BH, HD, HD]),
                                   rv.unsqueeze(1).to_broadcast([BH, HD, HD]), ALU.mult))
            dve.scalar_tensor_tensor(out=s0[:], in0=s0[:], scalar=gamma[:], in1=prod[:],
                                     op0=ALU.mult, op1=ALU.add).then_inc(s_state, 1)
            step(dve.tensor_reduce(st[:, 13:14], o[:], AX, ALU.add))
            step(dve.tensor_scalar(st[:, 13:14], st[:, 13:14], -1.0 / HD, None, ALU.mult))
            step(dve.tensor_scalar(o[:], o[:], st[:, 13:14], None, ALU.add))
            step(dve.tensor_tensor_reduce(sq[:, 0, :], o[:], o[:], 1.0, 0.0, ALU.mult, ALU.add, st[:, 14:15]))
            dve.tensor_scalar(st[:, 8:9], st[:, 14:15], 1.0 / HD, EPS, ALU.mult, ALU.add).then_inc(s_var, 1)
            dve.wait_ge(s_std, 3)
            step(dve.reciprocal(st[:, 10:11], st[:, 9:10]))
            step(dve.scalar_tensor_tensor(out=o[:], in0=o[:], scalar=st[:, 10:11], in1=gret[:],
                                          op0=ALU.mult, op1=ALU.mult))
            dve.wait_ge(s_silu, 1)
            step(dve.tensor_tensor(mix[:, 0, :], o[:], srg[:], ALU.mult))
            J = NSEL // LOTS
            for n in range(LOTS):
                dve.wait_ge(s_kv[n % 2], 16 * (n // 2 + 1))
                kk = kv[n % 2][:].rearrange("p (j d) -> p j d", d=HD)
                step(dve.tensor_tensor(kk, kk, aq.unsqueeze(1).to_broadcast([BH, J, HD]), ALU.mult))
                dve.tensor_reduce(S[:, n * J:(n + 1) * J], kk, AX, ALU.add).then_inc(s_kvu, 1)
            dve.wait_ge(s_kvu, LOTS)
            step(dve.tensor_tensor_reduce(sq[:, 0, :], aq, ak, 1.0, 0.0, ALU.mult, ALU.add, S[:, NSEL:NSEL + 1]))
            step(dve.tensor_tensor_reduce(S[:], S[:], bias[:], 1.0, LOWEST, ALU.add, ALU.max, st[:, 15:16]))
            dve.tensor_scalar(st[:, 11:12], st[:, 15:16], -1.0, None, ALU.mult).then_inc(s_max, 1)
            dve.wait_ge(s_exp, 1)
            step(dve.tensor_tensor_reduce(S[:], S[:], count[:], 1.0, 0.0, ALU.mult, ALU.add, st[:, 0:1]))
            step(dve.reciprocal(st[:, 1:2], st[:, 0:1]))
            for n in range(LOTS):
                m, E = n + LOTS, HD // LOTS
                dve.wait_ge(s_kv[m % 2], 16 * (m // 2 + 1))
                vv = kv[m % 2][:].rearrange("p (e j) -> p e j", j=NSEL)
                step(dve.tensor_tensor(vv, vv, S[:, 0:NSEL].unsqueeze(1).to_broadcast([BH, E, NSEL]), ALU.mult))
                dve.tensor_reduce(osum[:, n * E:(n + 1) * E], vv, AX, ALU.add).then_inc(s_kvu, 1)
            dve.wait_ge(s_kvu, 2 * LOTS)
            step(dve.scalar_tensor_tensor(out=osum[:], in0=av, scalar=S[:, NSEL:NSEL + 1], in1=osum[:],
                                          op0=ALU.mult, op1=ALU.add))
            dve.tensor_scalar(mix[:, 1, :], osum[:], st[:, 1:2], None, ALU.mult).then_inc(s_mix, 1)
            dve.wait_ge(s_mT, 1)
            dve.tensor_copy(mixTs[:], psO[1][:, 0:KT * B].rearrange("p (k b) -> p k b", b=B)).then_inc(s_mTc, 1)
            dve.wait_ge(s_wo, 2)
            step(dve.tensor_tensor(xms[:], psS[0][0:B, :], rows[:, 0, :], ALU.mult))
            dve.tensor_tensor(xms[:], xms[:], xs[:], ALU.add).then_inc(s_h2, 1)
            dve.wait_ge(s_h2, 1)
            norm(xms, 4)
            step(dve.scalar_tensor_tensor(out=h2s[:], in0=xms[:], scalar=stB[:, 3:4], in1=rows[:, 1, :],
                                          op0=ALU.mult, op1=ALU.mult))
            dve.tensor_tensor(h2s[:], h2s[:], rows[:, 2, :], ALU.add).then_inc(s_h2, 1)


def peer(nc, a, sem, ps, psS, psO, ident, gt2row):
    with ExitStack() as ctx:
        def sb(name, shape, dt=F32):
            return ctx.enter_context(nc.sbuf_tensor("pr_" + name, shape, dt))

        wpq = sb("wpq", [P, KT, HP * P])
        subk = sb("subk", [P, HP, 2 * NK])
        iota = sb("iota", [P, TOPK])
        ring = [sb(f"ring{i}", [P, 2 * D]) for i in range(RING)]
        h2cur = sb("h2cur", [P, D])
        h2next = sb("h2next", [P, D])
        h2T = sb("h2T", [P, KT, P])
        xmid = sb("xmid", [P, D])
        ysum = sb("ysum", [P, D])
        diag = sb("diag", [P, TOPK, P])
        zeros = sb("zeros", [P, P])
        qh = sb("qh", [P, P])
        qhT = sb("qhT", [P, P])
        sc = sb("sc", [P, 2 * NK])
        work = sb("work", [P, 256])
        cand = sb("cand", [P, TOPK, TOPK])
        top = sb("top", [P, 3, TOPK])
        pos = sb("pos", [P, 3, TOPK], U32)
        half_pos = sb("half_pos", [P, 2, TOPK], U32)
        half_f = sb("half_f", [P, 2, TOPK])
        key_f = sb("key_f", [P, 2, TOPK])
        hit = sb("hit", [P, TOPK, TOPK])
        pick = sb("pick", [P, 2, TOPK])
        expert_f = sb("expert_f", [P, SLOTS])
        expert = sb("expert", [P, SLOTS], U32)
        delta = sb("delta", [P, SLOTS])
        expert_h = [sb(f"expert_h{i}", [P, TOPK], U32) for i in range(2)]
        gate_h = sb("gate_h", [P, TOPK])
        dot = sb("dot", [P, TOPK])
        act_h = sb("act_h", [P, TOPK])
        small = sb("small", [P, 4])
        expT = sb("expT", [P, B], U32)
        gateT = sb("gateT", [P, B])
        gates = sb("gates", [P, SLOTS])
        gsum = sb("gsum", [P, HP])
        coef = sb("coef", [P, B, B])
        h2b = [sb(f"h2b{i}", [P, D]) for i in range(2)]
        gt2s = sb("gt2s", [B, D])

        s_w = sem("peer_weights")
        s_set = sem("peer_buffers_set")
        s_h2 = sem("h2_loaded")
        s_cur = sem("h2_current")
        s_hT = sem("h2_turned")
        s_hTc = sem("h2_turned_copied")
        s_qh = sem("peer_query")
        s_qhc = sem("peer_query_copied")
        s_qT = sem("peer_query_turned")
        s_qTc = sem("peer_query_turned_copied")
        s_sc = sem("peer_scores")
        s_scc = sem("peer_scores_copied")
        s_top = sem("experts_chosen")
        s_ixh = sem("expert_indices_placed")
        s_g = [sem(f"gathered{i}") for i in range(RING)]
        s_dh = sem("gate_scores_placed")
        s_ge = sem("gates_exp")
        s_dot = sem("dots")
        s_gelu = sem("gelu")
        s_coef = sem("expert_weights")
        s_dg = sem("diagonals")
        s_free = sem("ring_free")
        s_y = sem("peer_summed")
        s_yc = sem("peer_sum_copied")
        s_xm = sem("x_mid_loaded")
        s_out = sem("y_ready")
        s_st = sem("y_stored")
        s_ch = sem("dve_peer_step")
        s_passed = sem("peer_wait_passed")
        s_h2b = [sem(f"h2_row_spread{i}") for i in range(2)]
        s_sT = sem("sample_turned")
        s_ys = sem("y_sample_stored")

        GROUPS = TOPK // GRP
        block = ctx.enter_context(nc.Block())

        @block.sync
        def _(sp):
            for begun in (s_out,):
                sp.sem_inc(begun, 1)
            sp.dma_start(h2next[:], a["h2"][0:P, :]).then_inc(s_h2, 16)
            sp.dma_start(wpq[:], a["w_pq"].rearrange("(k p) n -> p k n", p=P)).then_inc(s_w, 16)
            sp.dma_start(subk[:], a["subk"]).then_inc(s_w, 16)
            sp.dma_start(iota[:], a["c_iota"]).then_inc(s_w, 16)
            sp.dma_start(gt2s[:], a["gt2_sample"]).then_inc(s_w, 16)
            with sp.Fori(0, T) as t:
                sp.wait_ge(s_cur, t + 1)
                sp.wait_ge(s_hT, t * 2 + 2)
                sp.dma_start(h2next[:], a["h2"][ds((t + 1) * P, P), :]).then_inc(s_h2, 16)
                sp.wait_ge(s_out, t + 1)
                sp.dma_start(xmid[:], a["x_mid"][ds(t * P, P), :]).then_inc(s_xm, 16)
                sp.wait_ge(s_out, t + 2)
                sp.dma_start(a["y_prompt"][ds(t * P, P), :], ysum[:]).then_inc(s_st, 16)
            sp.dma_start(xmid[0:B, :], a["x_mid"][T * P:T * P + B, :]).then_inc(s_xm, 16)
            for b in range(B):
                if b >= 2:
                    sp.wait_ge(s_dot, T * HP * GROUPS + b - 1)
                row = a["h2"][T * P + b:T * P + b + 1, :].to_broadcast([P, D])
                sp.dma_start(h2b[b % 2][:], row).then_inc(s_h2b[b % 2], 16)
            sp.wait_ge(s_out, T + 2)
            sp.dma_start(a["y_sample"], ysum[0:B, :]).then_inc(s_ys, 16)
            sp.wait_ge(s_ys, 16)
            sp.wait_ge(s_st, 16 * T + 1)

        @block.gpsimd
        def _(pool):
            with pool.Fori(0, T) as t:
                with pool.Fori(0, HP // 2) as hh:
                    for u in range(2):
                        n = t * HP + hh * 2 + u
                        pool.wait_ge(s_top, n + 2)
                        pool.tensor_copy(expert_h[u][:], expert[:, ds((hh * 2 + u) * TOPK, TOPK)]).then_inc(s_ixh, 1)
                        pool.wait_ge(s_ixh, n + 1)
                        for s in range(TOPK):
                            if s % GRP == 0:
                                pool.wait_ge(s_free, n * GROUPS + s // GRP + 1)
                                pool.sem_inc(s_passed, 1)
                            r = s % RING
                            pool.indirect_dma_start(
                                ring[r][:], None, a["uv"],
                                bass.IndirectOffsetOnAxis(ap=expert_h[u][:, s:s + 1], axis=0)).then_inc(s_g[r], 16)
            pool.wait_ge(s_sT, 3)
            for b in range(B):
                if b == 0:
                    pool.wait_ge(s_free, T * HP * GROUPS + RING // GRP)
                pool.indirect_dma_start(
                    ring[b][:], None, a["uv"],
                    bass.IndirectOffsetOnAxis(ap=expT[:, b:b + 1], axis=0)).then_inc(s_g[b], 16)

        @block.scalar
        def _(act):
            for begun in (s_top, s_st):
                act.sem_inc(begun, 1)
            def turned(i):
                for half in range(2):
                    act.wait_ge(s_hT, i * 2 + half + 1)
                    act.activation(h2T[:, half * 4:half * 4 + 4, :],
                                   psS[1][:, half * 512:half * 512 + 512].rearrange("p (g i) -> p g i", g=4),
                                   ACT.Copy).then_inc(s_hTc, 1)

            def scores(n):
                act.wait_ge(s_qh, n + 1)
                act.activation(qh[:], ps[0][:, 0:P], ACT.Copy).then_inc(s_qhc, 1)
                act.wait_ge(s_qT, n + 1)
                act.activation(qhT[:], ps[1][:, 0:P], ACT.Copy).then_inc(s_qTc, 1)
                act.wait_ge(s_sc, n + 1)
                act.wait_ge(s_top, n + 1)
                act.activation(sc[:], psO[0][:, 0:2 * NK], ACT.Copy).then_inc(s_scc, 1)

            turned(0)
            with act.Fori(0, HP) as h:
                scores(h)
            with act.Fori(0, T) as t:
                turned(t + 1)
                with act.Fori(0, HP) as h:
                    n = t * HP + h
                    act.wait_ge(s_dh, n + 1)
                    act.activation(gate_h[:], gate_h[:], ACT.Exp, accum_out=small[:, 0:1]).then_inc(s_ge, 1)
                    scores(n + HP)
                    for q in range(GROUPS):
                        act.wait_ge(s_dot, n * GROUPS + q + 1)
                        c = slice(q * GRP, q * GRP + GRP)
                        act.activation(act_h[:, c], dot[:, c], ACT.Gelu).then_inc(s_gelu, 1)
                act.wait_ge(s_y, t + 1)
                act.wait_ge(s_st, t * 16 + 1)
                act.activation(ysum[:], psS[0][:], ACT.Copy).then_inc(s_yc, 1)
            act.wait_ge(s_dh, T * HP + 1)
            act.activation(gates[:], delta[:], ACT.Exp).then_inc(s_ge, 1)
            for b in range(B):
                act.wait_ge(s_dot, T * HP * GROUPS + b + 1)
                act.activation(act_h[:, b:b + 1], dot[:, b:b + 1], ACT.Gelu).then_inc(s_gelu, 1)

        @block.tensor
        def _(pe):
            for begun in (s_qhc, s_scc, s_yc):
                pe.sem_inc(begun, 1)
            def turn():
                for half in range(2):
                    for j in range(4):
                        k = half * 4 + j
                        last = pe.transpose(psS[1][:, k * P:(k + 1) * P], h2next[:, k * P:(k + 1) * P], ident[:])
                    last.then_inc(s_hT, 1)

            def scores(h, n):
                pe.wait_ge(s_qhc, n + 1)
                for k in range(KT):
                    last = pe.matmul(ps[0][:, 0:P], h2T[:, k, :], wpq[:, k, ds(h * P, P)],
                                     start=(k == 0), stop=(k == KT - 1))
                last.then_inc(s_qh, 1)
                pe.wait_ge(s_qhc, n + 2)
                pe.transpose(ps[1][:, 0:P], qh[:], ident[:]).then_inc(s_qT, 1)
                pe.wait_ge(s_qTc, n + 1)
                pe.wait_ge(s_scc, n + 1)
                pe.matmul(psO[0][:, 0:2 * NK], qhT[:], subk[:, ds(h, 1), :].rearrange("p o k -> p (o k)"),
                          start=True, stop=True).then_inc(s_sc, 1)

            pe.wait_ge(s_h2, 16)
            turn()
            pe.wait_ge(s_w, 64)
            pe.wait_ge(s_hTc, 2)
            with pe.Fori(0, HP) as h:
                scores(h, h)
            pe.wait_ge(s_set, 2)
            with pe.Fori(0, T) as t:
                pe.wait_ge(s_yc, t + 1)
                for half in range(2):
                    pe.matmul(psS[0][:, half * 512:half * 512 + 512], zeros[:], wpq[:, 0, 0:512],
                              start=True, stop=False, skip_group_check=True)
                pe.wait_ge(s_h2, t * 16 + 32)
                turn()
                pe.wait_ge(s_hTc, t * 2 + 4)
                pe.sem_inc(s_passed, 1)
                with pe.Fori(0, HP) as h:
                    n = t * HP + h
                    scores(h, n + HP)
                    for q in range(GROUPS):
                        pe.wait_ge(s_dg, n * GROUPS + q + 1)
                        for s in range(q * GRP, q * GRP + GRP):
                            for half in range(2):
                                last = pe.matmul(psS[0][:, half * 512:half * 512 + 512], diag[:, s, :],
                                                 ring[s % RING][:, D + half * 512:D + half * 512 + 512],
                                                 start=False, stop=False, skip_group_check=True)
                        last.then_inc(s_free, 1)
                for half in range(2):
                    last = pe.matmul(psS[0][:, half * 512:half * 512 + 512], zeros[:], wpq[:, 0, 0:512],
                                     start=False, stop=True, skip_group_check=True)
                last.then_inc(s_y, 1)
            pe.wait_ge(s_top, HP * (T + 1) + 1)
            pe.transpose(ps[0][:, 0:P], expert_f[:], ident[:]).then_inc(s_sT, 1)
            pe.wait_ge(s_dh, T * HP + 2)
            pe.transpose(ps[1][:, 0:P], gates[:], ident[:]).then_inc(s_sT, 1)
            pe.wait_ge(s_yc, T + 1)
            for b in range(B):
                pe.wait_ge(s_dg, T * HP * GROUPS + b + 1)
                for half in range(2):
                    last = pe.matmul(psS[0][0:B, half * 512:half * 512 + 512], coef[:, b, :],
                                     ring[b][:, D + half * 512:D + half * 512 + 512],
                                     start=(b == 0), stop=(b == B - 1), skip_group_check=True)
            last.then_inc(s_y, 1)

        @block.vector
        def _(dve):
            steps = [0]

            def step(ins):
                steps[0] += 1
                ins.then_inc(s_ch, 1)
                dve.wait_ge(s_ch, steps[0])

            def restart():
                dve.sem_clear(s_ch)
                steps[0] = 0

            def best8(m, ix, values, n):
                step(dve.max(m[:, 0:8], values))
                step(dve.match_replace(work[:, 0:n], m[:, 0:8], values, LOWEST))
                step(dve.max_index(ix[:, 0:8], m[:, 0:8], values))

            def next8(m, ix, n):
                step(dve.max(m[:, 8:16], work[:, 0:n]))
                step(dve.max_index(ix[:, 8:16], m[:, 8:16], work[:, 0:n]))

            def choose(part, h, n):
                if part in (1, 2):
                    c = part - 1
                    if c == 0:
                        dve.wait_ge(s_scc, n + 2)
                        dve.sem_inc(s_passed, 1)
                    best8(top[:, c, :], pos[:, c, :], sc[:, c * NK:(c + 1) * NK], NK)
                    next8(top[:, c, :], pos[:, c, :], NK)
                if part == 3:
                    step(dve.tensor_tensor(cand[:], top[:, 0, :].unsqueeze(2).to_broadcast([P, TOPK, TOPK]),
                                           top[:, 1, :].unsqueeze(1).to_broadcast([P, TOPK, TOPK]), ALU.add))
                    best8(top[:, 2, :], pos[:, 2, :], cand[:].rearrange("p a b -> p (a b)"), TOPK * TOPK)
                if part == 4:
                    next8(top[:, 2, :], pos[:, 2, :], TOPK * TOPK)
                    step(dve.tensor_scalar(half_pos[:, 0, :], pos[:, 2, :], 4, None, ALU.logical_shift_right))
                    step(dve.tensor_scalar(half_pos[:, 1, :], pos[:, 2, :], TOPK - 1, None, ALU.bitwise_and))
                    step(dve.tensor_copy(half_f[:], half_pos[:]))
                    step(dve.tensor_copy(key_f[:], pos[:, 0:2, :]))
                if part in (5, 6):
                    c = part - 5
                    step(dve.tensor_tensor(hit[:], half_f[:, c, :].unsqueeze(2).to_broadcast([P, TOPK, TOPK]),
                                           iota[:].unsqueeze(1).to_broadcast([P, TOPK, TOPK]), ALU.is_equal))
                    step(dve.tensor_tensor(hit[:], hit[:],
                                           key_f[:, c, :].unsqueeze(1).to_broadcast([P, TOPK, TOPK]), ALU.mult))
                    step(dve.tensor_reduce(pick[:, c, :], hit[:], AX, ALU.add))
                if part == 7:
                    at = ds(h * TOPK, TOPK)
                    step(dve.tensor_scalar(delta[:, at], top[:, 2, :], top[:, 2, 0:1], None, ALU.subtract))
                    step(dve.scalar_tensor_tensor(out=expert_f[:, at], in0=pick[:, 0, :], scalar=float(NK),
                                                  in1=pick[:, 1, :], op0=ALU.mult, op1=ALU.add))
                    dve.tensor_copy(expert[:, at], expert_f[:, at]).then_inc(s_top, 1)

            PARTS = 8
            assert PARTS == GROUPS
            dve.memset(zeros[:], 0.0).then_inc(s_set, 1)
            dve.memset(coef[:], 0.0).then_inc(s_set, 1)
            dve.memset(small[:, 1:2], 0.0).then_inc(s_free, RING // GRP)
            dve.wait_ge(s_w, 64)
            with dve.Fori(0, HP) as h:
                restart()
                for part in range(PARTS):
                    choose(part, h, h)

            with dve.Fori(0, T) as t:
                dve.wait_ge(s_h2, t * 16 + 16)
                dve.tensor_copy(h2cur[:], h2next[:]).then_inc(s_cur, 1)
                dve.wait_ge(s_cur, t + 1)
                dve.sem_inc(s_passed, 1)
                with dve.Fori(0, HP) as h:
                    n = t * HP + h
                    restart()
                    dve.tensor_copy(gate_h[:], delta[:, ds(h * TOPK, TOPK)]).then_inc(s_dh, 1)
                    for q in range(GROUPS):
                        for s in range(q * GRP, q * GRP + GRP):
                            r = s % RING
                            dve.wait_ge(s_g[r], (n * (TOPK // RING) + s // RING) * 16 + 16)
                            last = dve.tensor_tensor_reduce(ring[r][:, 0:D], ring[r][:, 0:D], h2cur[:], 1.0, 0.0,
                                                            ALU.mult, ALU.add, dot[:, s:s + 1])
                        last.then_inc(s_dot, 1)
                        if q == 0:
                            dve.wait_ge(s_ge, n + 1)
                            step(dve.reciprocal(small[:, 1:2], small[:, 0:1]))
                        dve.wait_ge(s_gelu, n * GROUPS + q + 1)
                        c = slice(q * GRP, q * GRP + GRP)
                        dve.scalar_tensor_tensor(out=act_h[:, c], in0=act_h[:, c], scalar=small[:, 1:2],
                                                 in1=gate_h[:, c], op0=ALU.mult, op1=ALU.mult).then_inc(s_coef, 1)
                        dve.wait_ge(s_coef, n * GROUPS + q + 1)
                        for s in range(q * GRP, q * GRP + GRP):
                            last = dve.tensor_scalar(diag[:, s, :], ident[:], act_h[:, s:s + 1], None, ALU.mult)
                        last.then_inc(s_dg, 1)
                        choose(q, h, n + HP)
                restart()
                dve.wait_ge(s_yc, t + 2)
                dve.wait_ge(s_xm, t * 16 + 16)
                step(dve.tensor_tensor(ysum[:], ysum[:], gt2row[:], ALU.mult))
                dve.tensor_tensor(ysum[:], ysum[:], xmid[:], ALU.add).then_inc(s_out, 1)
            restart()
            dve.wait_ge(s_top, HP * (T + 1) + 1)
            dve.tensor_copy(small[:, 2:3], delta[:, 0:1]).then_inc(s_dh, 1)
            dve.wait_ge(s_ge, T * HP + 1)
            g3 = gates[:].rearrange("p (h k) -> p h k", k=TOPK)
            step(dve.tensor_reduce(gsum[:], g3, AX, ALU.add))
            step(dve.reciprocal(gsum[:], gsum[:]))
            dve.tensor_tensor(g3, g3, gsum[:].unsqueeze(2).to_broadcast([P, HP, TOPK]), ALU.mult).then_inc(s_dh, 1)
            dve.wait_ge(s_sT, 1)
            dve.tensor_copy(expT[:], ps[0][:, 0:B]).then_inc(s_sT, 1)
            dve.wait_ge(s_sT, 3)
            step(dve.tensor_copy(gateT[:], ps[1][:, 0:B]))
            for b in range(B):
                dve.wait_ge(s_g[b], (T * HP * (TOPK // RING)) * 16 + 16)
                dve.wait_ge(s_h2b[b % 2], 16 * (b // 2 + 1))
                dve.tensor_tensor_reduce(ring[b][:, 0:D], ring[b][:, 0:D], h2b[b % 2][:], 1.0, 0.0,
                                         ALU.mult, ALU.add, dot[:, b:b + 1]).then_inc(s_dot, 1)
                dve.wait_ge(s_gelu, T * HP * GROUPS + b + 1)
                dve.tensor_scalar(coef[:, b, b:b + 1], act_h[:, b:b + 1], gateT[:, b:b + 1], None, ALU.mult)\
                   .then_inc(s_dg, 1)
            dve.wait_ge(s_y, T + 1)
            dve.wait_ge(s_st, 16 * T + 1)
            dve.wait_ge(s_xm, 16 * (T + 1))
            step(dve.tensor_tensor(ysum[0:B, :], psS[0][0:B, :], gt2s[:], ALU.mult))
            dve.tensor_tensor(ysum[0:B, :], ysum[0:B, :], xmid[0:B, :], ALU.add).then_inc(s_out, 1)


def _constants():
    f = np.float64
    c = {"c_ident": np.eye(P)}
    c["c_iota"] = np.tile(np.arange(TOPK, dtype=f), (P, 1))

    def counts(d):
        inside = [(d >= 0) & (d <= window) & (d % dil == 0) for window, dil in BRANCHES]
        return np.sum(inside, axis=0).astype(f)

    p, col = np.arange(P)[:, None], np.arange(SPAN)[None, :]
    d = p + (T - 1) * P - col
    c["c_dist"] = np.where(counts(d) > 0, -d, MASKED)
    d = (T - 1 - col // P) * P + col % P - p
    c["c_count"] = counts(d)
    log_decay = np.log1p(-np.exp2(-5.0 - np.arange(H, dtype=f)))
    i = np.arange(P)
    diff = i[None, :] - i[:, None]
    c["c_intra"] = np.concatenate([np.where(diff >= 0, np.exp(np.maximum(diff, 0) * g), 0) * HD ** -0.5
                                   for g in np.concatenate([log_decay[0::2], log_decay[1::2]])], axis=1)
    pair = np.exp((i + 1)[None, None, :] * log_decay.reshape(G, 2, 1))
    c["c_wstart"] = np.repeat(pair.transpose(1, 0, 2), HD, axis=0).reshape(P, G * P)
    c["c_wend"] = np.exp((P - 1 - i)[:, None] * log_decay[None, :]) * HD ** -0.5
    c["c_cdecay"] = np.repeat(np.exp(P * log_decay).reshape(G, 2).T, HD, axis=0)
    slopes = np.exp2(-(np.arange(H) + 1.0))
    c["c_qkscale"] = np.tile(np.concatenate([HD ** -0.5 / slopes, np.ones(H)]), (P, 1))
    age = np.array(_selected_ages() + [0])
    c["c_bias_s"] = np.tile(-slopes[:, None] * age[None, :], (B, 1))
    c["c_count_s"] = np.tile(counts(age)[None, :], (B * H, 1))
    c["c_gamma"] = np.tile(np.exp(log_decay)[:, None], (B, 1))
    return {k: np.ascontiguousarray(v, np.float32) for k, v in c.items()}


def _selected_ages():
    ages = [g for g in range(1, PAST + 1) if any(g <= w and g % d == 0 for w, d in BRANCHES)]
    assert len(ages) == NSEL
    return ages


def _layout(x):
    z = {k: np.asarray(v) for k, v in x.items()}
    r = {"x_sample": z["x_sample"][:, 0]}
    r["x_all"] = np.concatenate([z["x_prompt"][0], np.zeros((P, D), np.float32)])
    c = np.concatenate([z["c_sample"], z["c_prompt"]], axis=0).T
    r["cT"] = c.reshape(KT, P, NC9).transpose(1, 0, 2)
    for n in ("w_ada", "w_in", "w_out", "w_pq"):
        r[n] = z[n][0]
    r["b_adaT"] = z["b_ada"][0].reshape(48, P).T
    r["gnT"] = np.stack([z["g_norm1"][0].reshape(KT, P).T, z["g_norm2"][0].reshape(KT, P).T], axis=1)
    r["g_qk"] = np.tile(np.concatenate([z["g_qn"][0].reshape(-1), z["g_kn"][0].reshape(-1)]), (P, 1))
    keys = np.zeros((P, HP, 2 * NK), np.float32)
    for c in range(2):
        keys[c * HD:(c + 1) * HD, :, c * NK:(c + 1) * NK] = z["sub_keys"][0, :, c].transpose(2, 0, 1)
    r["subk"] = keys
    r["uv"] = np.concatenate([z["peer_u"][0], z["peer_v"][0]], axis=1)
    r["state_s"] = z["state_ret"][0].reshape(B * H, HD, HD)
    rows = PAST - np.array(_selected_ages())
    r["k_sel"] = z["cache_win_k"][0][:, rows].transpose(0, 2, 1, 3).reshape(B * H, NSEL * HD)
    r["v_sel"] = z["cache_win_v"][0][:, rows].transpose(0, 2, 3, 1).reshape(B * H, HD * NSEL)
    r["g_qk_s"] = np.tile(np.stack([z["g_qn"][0], z["g_kn"][0]], axis=1), (B, 1, 1))
    r["g_ret_s"] = np.tile(z["g_ret"][0], (B, 1))
    r["g_ret_rows"] = np.tile(z["g_ret"][0].reshape(-1), (P, 1))
    return r


_OUTS = {"y_prompt": (1024, D), "y_sample": (B, D), "ret_prompt": (H * HD, HD), "wk_prompt": (1024, HW),
         "wv_prompt": (1024, HW), "ret_sample": (B * H, HD * HD), "wk_sample": (B * H, HD), "wv_sample": (B * H, HD)}
_SCRATCH = {"x_mid": ((T + 1) * P, D), "h2": ((T + 1) * P, D), "gt2_sample": (B, D), "proj_s": (NPROJ, B, HW), "mix_s": (B * H, 2 * HD)}


def kernel(**inputs):
    import concourse.bacc as bacc
    from concourse.bass_utils import run_bass_kernel_spmd as run

    nc = bacc.Bacc("TRN2", target_bir_lowering=False, num_devices=1)
    arrays, aps = {}, {}
    for name, v in {**_layout(inputs), **_constants()}.items():
        arrays[name] = np.ascontiguousarray(v)
        aps[name] = nc.dram_tensor(name, v.shape, F32, kind="ExternalInput").ap()
    for name, shape in _OUTS.items():
        aps[name] = nc.dram_tensor(name, shape, F32, kind="ExternalOutput").ap()
    for name, shape in _SCRATCH.items():
        aps[name] = nc.dram_tensor(name, shape, F32, kind="Internal").ap()
    build(nc, aps)
    got = run(nc, [arrays], core_ids=[0]).results[0]
    hd = (H, HD)
    return (got["y_prompt"].reshape(1, 1024, D), got["y_sample"].reshape(B, 1, D),
            got["ret_prompt"].reshape(1, 1, H, HD, HD), got["wk_prompt"].reshape(1, 1, 1024, *hd),
            got["wv_prompt"].reshape(1, 1, 1024, *hd), got["ret_sample"].reshape(1, B, H, HD, HD),
            got["wk_sample"].reshape(1, B, 1, *hd), got["wv_sample"].reshape(1, B, 1, *hd))
```

```python
from contextlib import ExitStack

import numpy as np

import concourse.bass as bass
from concourse import mybir

F32 = mybir.dt.float32
U32 = mybir.dt.uint32
ALU = mybir.AluOpType
ACT = mybir.ActivationFunctionType
AX = mybir.AxisListType.X
ds = bass.ds

P = 128
D = 1024
KT = D // P
T = 1024 // P
B = 8
NC9 = B + 1
H = 8
HD = 64
HW = H * HD
G = H // 2
VA = HD + 1
SPAN = 2 * 1024 - P
NPROJ = 7
CHUNKS = NPROJ + 2
SEG = 2
WBUF = 3
ORDER = (4, 5, 0, 1, 2, 3, 6)
EPS = 1e-6
MASKED = -1e30
LOWEST = -3e38
HP = 8
TOPK = 16
NK = 128
SLOTS = HP * TOPK
RING = 8
GRP = 2
PAST = 1024
BRANCHES = ((128, 1), (512, 4), (2048, 16))
NSEL = 256
ADA_COLS = 512
ADA_CHUNKS = 6 * D // ADA_COLS


def halves(keys):
    return [slice(0, 512), slice(512, keys)] if keys > 512 else [slice(0, keys)]


def build(nc, a):
    with ExitStack() as whole:
        def sem(name):
            return whole.enter_context(nc.semaphore(name))

        ps = [whole.enter_context(nc.psum_tensor(f"bank{i}", [P, 512], F32)) for i in range(2)]
        psS = [whole.enter_context(nc.psum_tensor(f"pair{i}", [P, 1024], F32)) for i in range(2)]
        psO = [whole.enter_context(nc.psum_tensor(f"bank{6 + i}", [P, 512], F32)) for i in range(2)]

        def keep(name, shape, dt=F32):
            return whole.enter_context(nc.sbuf_tensor("sb_" + name, shape, dt))

        ident = keep("ident", [P, P])
        mod = keep("mod", [P, 48, NC9])
        gt2row = keep("gt2row", [P, D])
        tabs = keep("tabs", [P, 6, KT, NC9])
        front(nc, a, sem, ps, psS, psO, ident, mod, gt2row, tabs)
        decode(nc, a, sem, ps, psS, psO, ident, tabs)
        peer(nc, a, sem, ps, psS, psO, ident, gt2row)


def front(nc, a, sem, ps, psS, psO, ident, mod, gt2row, tabs):
    with ExitStack() as ctx:
        def sb(name, shape, dt=F32):
            return ctx.enter_context(nc.sbuf_tensor("sb_" + name, shape, dt))

        w = [sb(f"w{i}", [P, KT, 512]) for i in range(WBUF)]
        dist = sb("dist", [P, SPAN])
        count = sb("count", [P, SPAN])
        dist_t = sb("dist_t", [P, 1024])
        count_t = sb("count_t", [P, 1024])
        intra = sb("intra", [P, H * P])
        wstart = sb("wstart", [P, G * P])
        wend = sb("wend", [P, H])
        cdecay = sb("cdecay", [P, G])
        qkscale = sb("qkscale", [P, 2 * H])
        grow = sb("grow", [P, 2 * HW])
        gret = sb("gret", [P, HW])
        badaT = sb("badaT", [P, 48])
        gnT = sb("gnT", [P, 2, KT])
        cT = sb("cT", [P, KT, NC9])
        ones = sb("ones", [P, P])
        gt1row = sb("gt1row", [P, D])
        a2row = sb("a2row", [P, D])
        b2row = sb("b2row", [P, D])
        kT = sb("kT", [P, G, 1024])
        va = sb("va", [P, T, H * VA])
        xt = sb("xt", [P, D])
        xn = sb("xn", [P, D])
        hT = sb("hT", [P, KT, P])
        qk = sb("qk", [P, 2 * HW])
        qkn = sb("qkn", [P, 2 * HW])
        rq, rk, rv, srg, av = (sb(n, [P, HW]) for n in ("rq", "rk", "rv", "srg", "av"))
        turned = sb("turned", [P, 4, G, P])
        rqT, rkT, aqT, qTw = (turned[:, i] for i in range(4))
        kw = sb("kw", [P, HW])
        sT = sb("sT", [P, H * P])
        state = sb("state", [P, G, P])
        osb = sb("osb", [P, HW])
        sp = [sb(f"sp{i}", [P, 1024]) for i in range(2)]
        pt = [sb(f"pt{i}", [P, 1024]) for i in range(2)]
        mix = sb("mix", [P, D])
        arow, diagonals = (rq, rk), (*sp, *pt)
        mixT = turned[:, 0:2].rearrange("p a g i -> p (a g) i")
        xm, h2, junk, xres = qk, sp[0], xn, mix
        st = sb("st", [P, 64])
        ss, var, std, rstd = (st[:, i:i + 1] for i in range(4))
        nmax = st[:, 8:16]
        rden = st[:, 16:24]
        st16 = sb("st16", [P, 4, 16])
        ssq, varq, stdq, rstdq = (st16[:, i, :] for i in range(4))
        mu = sb("mu", [P, H])

        s_c = sem("conditioning_loaded")
        s_ident = sem("identity_loaded")
        s_const = sem("const_loaded")
        s_arow = sem("ada_rows_copied")
        s_adaT = sem("ada_rows_turned")
        s_tabs = sem("ada_tables")
        s_ada = [sem(f"ada_chunk{i}") for i in range(WBUF)]
        s_w = [sem(f"weight_chunk{i}") for i in range(WBUF)]
        s_silu = sem("silu_c")
        s_adamm = sem("ada_product")
        s_diag = sem("ada_diagonal")
        s_bc = sem("ada_broadcast")
        s_row = sem("ada_rows")
        s_init = sem("front_buffers_set")
        s_x = sem("x_loaded")
        s_xres = sem("residual_loaded")
        s_var = sem("variance")
        s_std = sem("deviation")
        s_xn = sem("x_normed")
        s_xT = sem("x_transposed")
        s_hT = sem("h_transposed")
        s_proj = sem("projected")
        s_evA = sem("projection_read_act")
        s_evD = sem("projection_read_dve")
        s_tr = sem("rows_transposed")
        s_te = sem("transposed_copied")
        s_qkn = sem("qk_normed")
        s_vaug = sem("values_placed")
        s_qTw = sem("q_decayed")
        s_kw = sem("k_decayed")
        s_rs = sem("ret_scores")
        s_sT = sem("ret_scores_decayed")
        s_oret = sem("ret_output")
        s_oread = sem("ret_output_read")
        s_state = sem("ret_state")
        s_S = sem("att_scores")
        s_nm = sem("att_max")
        s_P = sem("att_probs")
        s_pt = sem("att_probs_transposed")
        s_PT = sem("att_probs_weighted")
        s_pv = sem("att_output")
        s_mix = sem("mixed")
        s_mT = sem("mix_transposed")
        s_mixT = sem("mix_transposed_copied")
        s_wo = sem("out_projected")
        s_xm = sem("x_mid_half")
        s_h2 = sem("h2_ready")
        s_chain = sem("dve_step")
        s_passed = sem("front_wait_passed")
        s_owk = sem("stored_wk")
        s_owv = sem("stored_wv")
        s_oxm = sem("stored_x_mid")
        s_oh2 = sem("stored_h2")
        s_stored = sem("tiles_stored")
        s_oret_out = sem("stored_state")

        consts = [(dist, "c_dist"), (count, "c_count"), (intra, "c_intra"),
                  (wstart, "c_wstart"), (wend, "c_wend"), (cdecay, "c_cdecay"), (qkscale, "c_qkscale"),
                  (grow, "g_qk"), (gret, "g_ret_rows"), (badaT, "b_adaT"), (gnT, "gnT")]
        w_ada = a["w_ada"].rearrange("(k p) n -> p k n", p=P)
        w_in = a["w_in"].rearrange("(k p) n -> p k n", p=P)
        w_out = a["w_out"].rearrange("(k p) n -> p k n", p=P)
        nbuf = CHUNKS // WBUF
        assert CHUNKS % WBUF == 0 and ADA_CHUNKS % WBUF == 0

        block = ctx.enter_context(nc.Block())

        @block.sync
        def _(sp_):
            for begun in (s_wo, s_evA):
                sp_.sem_inc(begun, 1)
            sp_.dma_start(cT[:], a["cT"]).then_inc(s_c, 16)
            sp_.dma_start(ident[:], a["c_ident"]).then_inc(s_ident, 16)
            for c in range(ADA_CHUNKS):
                if c >= WBUF:
                    sp_.wait_ge(s_adamm, c - WBUF + 1)
                sp_.dma_start(w[c % WBUF][:], w_ada[:, :, c * 512:(c + 1) * 512]).then_inc(s_ada[c % WBUF], 16)
                if c == 2:
                    for tile, name in consts:
                        sp_.dma_start(tile[:], a[name]).then_inc(s_const, 16)
                    sp_.dma_start(xt[:], a["x_all"][0:P, :]).then_inc(s_x, 16)
            sp_.wait_ge(s_adamm, ADA_CHUNKS)
            with sp_.Fori(0, T) as t:
                for c in range(CHUNKS):
                    if 1 <= c < WBUF:
                        sp_.wait_ge(s_wo, t * 2 + 1)
                    elif c >= WBUF:
                        sp_.wait_ge(s_proj, t * NPROJ + c - WBUF + 1)
                    else:
                        sp_.wait_ge(s_evA, t * 5 + 1)
                    src = (w_in[:, :, ORDER[c] * HW:(ORDER[c] + 1) * HW] if c < NPROJ
                           else w_out[:, :, (c - NPROJ) * 512:(c - NPROJ + 1) * 512])
                    sp_.dma_start(w[c % WBUF][:], src).then_inc(s_w[c % WBUF], 16)
                    if c == WBUF:
                        sp_.wait_ge(s_xn, t + 1)
                        sp_.dma_start(xt[:], a["x_all"][ds((t + 1) * P, P), :]).then_inc(s_x, 16)
                sp_.wait_ge(s_mT, t * 2 + 2)
                sp_.dma_start(xres[:], a["x_all"][ds(t * P, P), :]).then_inc(s_xres, 16)

        @block.gpsimd
        def _(pool):
            pool.sem_inc(s_stored, 1)
            pool.memset(ones[:], 1.0).then_inc(s_init, 1)
            pool.memset(kT[:], 0.0).then_inc(s_init, 1)
            pool.memset(va[:], 1.0).then_inc(s_init, 1)
            pool.memset(state[:], 0.0).then_inc(s_init, 1)
            with pool.Fori(0, T) as t:
                row = ds(t * P, P)
                pool.wait_ge(s_qkn, t + 1)
                pool.sem_inc(s_passed, 1)
                pool.dma_start(a["wk_prompt"][row, :], qkn[:, HW:2 * HW]).then_inc(s_owk, 16)
                pool.wait_ge(s_evA, t * 5 + 6)
                pool.sem_inc(s_passed, 1)
                pool.dma_start(a["wv_prompt"][row, :], av[:]).then_inc(s_owv, 16)
                pool.wait_ge(s_h2, t + 1)
                pool.sem_inc(s_passed, 1)
                pool.dma_start(a["x_mid"][row, :], xm[:]).then_inc(s_oxm, 16)
                pool.dma_start(a["h2"][row, :], h2[:]).then_inc(s_oh2, 16)
                for out in (s_owk, s_owv, s_oxm, s_oh2):
                    pool.wait_ge(out, t * 16 + 16)
                pool.sem_inc(s_stored, 1)
            pool.wait_ge(s_state, 2 * T + 1)
            ret = a["ret_prompt"].rearrange("(g e d) f -> e d g f", e=2, d=HD)
            for e in range(2):
                pool.dma_start(ret[e], state[e * HD:(e + 1) * HD, :, e * HD:(e + 1) * HD]).then_inc(s_oret_out, 16)
            pool.wait_ge(s_oret_out, 32)

        @block.scalar
        def _(act):
            act.wait_ge(s_c, 16)
            act.activation(cT[:], cT[:], ACT.Silu).then_inc(s_silu, 1)
            for c in range(ADA_CHUNKS):
                act.wait_ge(s_adamm, c + 1)
                if c >= 2:
                    act.wait_ge(s_adaT, c - 1)
                act.activation(arow[c % 2][0:NC9, :], ps[c % 2][0:NC9, :], ACT.Copy).then_inc(s_arow, 1)

            def x_turned(n):
                for half in range(2):
                    act.wait_ge(s_xT, n * 2 + half + 1)
                    for j in range(4):
                        k = half * 4 + j
                        last = act.activation(hT[:, k, :], psS[1][:, k * P:(k + 1) * P], ACT.Identity,
                                              scale=tabs[:, 0, k, B:B + 1], bias=tabs[:, 1, k, B:B + 1])
                    last.then_inc(s_hT, 1)

            act.wait_ge(s_var, 1)
            act.activation(std, var, ACT.Sqrt).then_inc(s_std, 1)
            act.wait_ge(s_tabs, 1)
            x_turned(0)
            for n, row in enumerate((gt1row, a2row, b2row, gt2row)):
                act.wait_ge(s_bc, n + 1)
                act.activation(row[:], psS[n % 2][:], ACT.Copy).then_inc(s_row, 1)
            for first in range(0, T, SEG):
                keys = (first + SEG) * P
                with act.Fori(first, first + SEG) as t:
                    def read(n, dst, src, func=ACT.Copy):
                        act.wait_ge(s_proj, t * NPROJ + n)
                        act.activation(dst[:], src, func).then_inc(s_evA, 1)

                    def copy_turned(n, out):
                        act.wait_ge(s_tr, t * 4 + n + 1)
                        act.activation(out, ps[n % 2][:].rearrange("p (g i) -> p g i", g=G), ACT.Copy).then_inc(s_te, 1)

                    read(3, rq, psS[0][:, 0:512])
                    read(4, rk, psS[0][:, 512:1024])
                    act.wait_ge(s_var, t * 4 + 2)
                    act.activation(stdq, varq, ACT.Sqrt).then_inc(s_std, 1)
                    read(5, rv, psS[1][:, 0:512])
                    copy_turned(0, rqT)
                    read(6, srg, psS[1][:, 512:1024], ACT.Silu)
                    copy_turned(1, rkT)
                    act.wait_ge(s_stored, t + 1)
                    read(7, av, psS[0][:, 0:512])
                    copy_turned(2, aqT)
                    copy_turned(3, kT[:, :, ds(t * P, P)])
                    for h in range(H):
                        act.wait_ge(s_nm, t * H + h + 1)
                        act.activation(sp[h % 2][:, 0:keys], sp[h % 2][:, 0:keys], ACT.Exp,
                                       bias=nmax[:, h:h + 1]).then_inc(s_P, 1)
                        if h == 2:
                            act.wait_ge(s_var, t * 4 + 3)
                            act.activation(stdq[:, 0:H], varq[:, 0:H], ACT.Sqrt).then_inc(s_std, 1)
                        if h == H - 2:
                            act.wait_ge(s_var, t * 4 + 4)
                            act.activation(std, var, ACT.Sqrt).then_inc(s_std, 1)
                    x_turned(t + 1)
                    for half in range(2):
                        act.wait_ge(s_mT, t * 2 + half + 1)
                        act.activation(mixT[:, half * 4:half * 4 + 4, :],
                                       ps[half][:].rearrange("p (g i) -> p g i", g=4), ACT.Copy).then_inc(s_mixT, 1)
                    act.wait_ge(s_var, t * 4 + 5)
                    act.activation(std, var, ACT.Sqrt).then_inc(s_std, 1)

        @block.vector
        def _(dve):
            steps = [0]

            def step(ins):
                steps[0] += 1
                ins.then_inc(s_chain, 1)
                dve.wait_ge(s_chain, steps[0])

            def restart():
                dve.sem_clear(s_chain)
                steps[0] = 0

            def x_variance(n):
                dve.wait_ge(s_x, n * 16 + 16)
                step(dve.tensor_tensor_reduce(junk[:], xt[:], xt[:], 1.0, 0.0, ALU.mult, ALU.add, ss))
                dve.tensor_scalar(var, ss, 1.0 / D, EPS, ALU.mult, ALU.add).then_inc(s_var, 1)

            def x_scale(count):
                dve.wait_ge(s_std, count)
                step(dve.reciprocal(rstd, std))
                dve.tensor_scalar(xn[:], xt[:], rstd, None, ALU.mult).then_inc(s_xn, 1)

            x_variance(0)
            x_scale(1)

            dve.wait_ge(s_adaT, ADA_CHUNKS)
            dve.wait_ge(s_const, 16 * len(consts))
            step(dve.tensor_tensor(mod[:], psO[1][:, 0:48 * NC9].rearrange("p (m c) -> p m c", c=NC9),
                                   badaT[:].unsqueeze(2).to_broadcast([P, 48, NC9]), ALU.add))
            sec = [mod[:, s * KT:(s + 1) * KT, :] for s in range(6)]
            for n, (sc, sh, gt) in enumerate(((1, 0, 2), (4, 3, 5))):
                gb = gnT[:, n, :].unsqueeze(2).to_broadcast([P, KT, NC9])
                step(dve.scalar_tensor_tensor(out=tabs[:, 3 * n, :, :], in0=sec[sc], scalar=1.0, in1=gb,
                                              op0=ALU.add, op1=ALU.mult))
                step(dve.tensor_copy(tabs[:, 3 * n + 1, :, :], sec[sh]))
                dve.tensor_copy(tabs[:, 3 * n + 2, :, :], sec[gt]).then_inc(s_tabs, 1)
            dve.wait_ge(s_tabs, 2)
            for n, sec_no in enumerate((2, 3, 4, 5)):
                dve.tensor_tensor(diagonals[n][:].rearrange("p (k i) -> p k i", k=KT),
                                  ident[:].unsqueeze(1).to_broadcast([P, KT, P]),
                                  tabs[:, sec_no, :, B:B + 1].to_broadcast([P, KT, P]), ALU.mult).then_inc(s_diag, 1)
            dve.wait_ge(s_init, 4)
            dve.wait_ge(s_row, 4)

            for first in range(0, T, SEG):
                keys = (first + SEG) * P
                with dve.Fori(first, first + SEG) as t:
                    restart()
                    off = (T - 1) * P - t * P
                    step(dve.tensor_copy(dist_t[:, 0:keys], dist[:, ds(off, keys)]))
                    step(dve.tensor_copy(count_t[:, 0:keys], count[:, ds(off, keys)]))
                    dve.wait_ge(s_stored, t + 1)
                    for n in range(2):
                        dve.wait_ge(s_proj, t * NPROJ + n + 1)
                        dve.tensor_copy(qk[:, n * HW:(n + 1) * HW], psS[1][:, n * 512:(n + 1) * 512]).then_inc(s_evD, 1)
                    dve.wait_ge(s_evD, t * 2 + 2)
                    step(dve.tensor_tensor(junk[:], qk[:], qk[:], ALU.mult))
                    step(dve.tensor_reduce(ssq, junk[:].rearrange("p (h d) -> p h d", d=HD), AX, ALU.add))
                    dve.tensor_scalar(varq, ssq, 1.0 / HD, EPS, ALU.mult, ALU.add).then_inc(s_var, 1)
                    dve.wait_ge(s_std, t * 4 + 2)
                    step(dve.reciprocal(rstdq, stdq))
                    step(dve.tensor_tensor(rstdq, rstdq, qkscale[:], ALU.mult))
                    step(dve.tensor_tensor(qk[:].rearrange("p (h d) -> p h d", d=HD),
                                           qk[:].rearrange("p (h d) -> p h d", d=HD),
                                           rstdq.unsqueeze(2).to_broadcast([P, 2 * H, HD]), ALU.mult))
                    dve.tensor_tensor(qkn[:], qk[:], grow[:], ALU.mult).then_inc(s_qkn, 1)
                    dve.wait_ge(s_evA, t * 5 + 3)
                    dve.tensor_tensor(kw[:].rearrange("p (h d) -> p h d", d=HD), rk[:].rearrange("p (h d) -> p h d", d=HD),
                                      wend[:].unsqueeze(2).to_broadcast([P, H, HD]), ALU.mult).then_inc(s_kw, 1)
                    dve.wait_ge(s_te, t * 4 + 1)
                    dve.tensor_tensor(qTw[:], rqT[:], wstart[:].rearrange("p (g i) -> p g i", g=G), ALU.mult)\
                       .then_inc(s_qTw, 1)
                    dve.wait_ge(s_evA, t * 5 + 6)
                    dve.tensor_copy(va[:, ds(t, 1), :].rearrange("p o (h e) -> p (o h) e", e=VA)[:, :, 0:HD],
                                    av[:].rearrange("p (h d) -> p h d", d=HD)).then_inc(s_vaug, 1)
                    for half in range(2):
                        dve.wait_ge(s_rs, t * 2 + half + 1)
                        c = slice(half * 512, half * 512 + 512)
                        dve.tensor_tensor(sT[:, c], psS[1][:, c], intra[:, c], ALU.mult).then_inc(s_sT, 1)
                    def att_max(h):
                        dve.wait_ge(s_S, t * H + h + 1)
                        if h >= 2:
                            dve.wait_ge(s_pt, t * 2 * H + 2 * (h - 2) + 2)
                        dve.sem_inc(s_passed, 1)
                        step(dve.tensor_tensor_reduce(sp[h % 2][:, 0:keys], psS[h % 2][:, 0:keys], dist_t[:, 0:keys],
                                                      2.0 ** -(h + 1), LOWEST,
                                                      ALU.add, ALU.max, nmax[:, h:h + 1]))
                        dve.tensor_scalar(nmax[:, h:h + 1], nmax[:, h:h + 1], -1.0, None, ALU.mult).then_inc(s_nm, 1)

                    def att_weigh(h):
                        if h >= 2:
                            dve.wait_ge(s_pv, t * H + h - 1)
                        for half, c in enumerate(halves(keys)):
                            dve.wait_ge(s_pt, t * 2 * H + 2 * h + half + 1)
                            dve.tensor_tensor(pt[h % 2][:, c], ps[half][:, 0:c.stop - c.start], count_t[:, c],
                                              ALU.mult).then_inc(s_PT, 2 // len(halves(keys)))

                    def groupnorm():
                        o3 = osb[:].rearrange("p (h d) -> p h d", d=HD)
                        j3 = junk[:, 0:HW].rearrange("p (h d) -> p h d", d=HD)
                        dve.wait_ge(s_oread, t + 1)
                        step(dve.tensor_reduce(mu[:], o3, AX, ALU.add))
                        step(dve.tensor_scalar(mu[:], mu[:], -1.0 / HD, None, ALU.mult))
                        step(dve.tensor_tensor(o3, o3, mu[:].unsqueeze(2).to_broadcast([P, H, HD]), ALU.add))
                        step(dve.tensor_tensor(j3, o3, o3, ALU.mult))
                        step(dve.tensor_reduce(ssq[:, 0:H], j3, AX, ALU.add))
                        dve.tensor_scalar(varq[:, 0:H], ssq[:, 0:H], 1.0 / HD, EPS, ALU.mult, ALU.add).then_inc(s_var, 1)

                    def gate():
                        o3 = osb[:].rearrange("p (h d) -> p h d", d=HD)
                        dve.wait_ge(s_std, t * 4 + 3)
                        step(dve.reciprocal(rstdq[:, 0:H], stdq[:, 0:H]))
                        step(dve.tensor_tensor(o3, o3, rstdq[:, 0:H].unsqueeze(2).to_broadcast([P, H, HD]), ALU.mult))
                        step(dve.tensor_tensor(osb[:], osb[:], gret[:], ALU.mult))
                        step(dve.tensor_tensor(mix[:].rearrange("p (h c) -> p h c", h=H)[:, :, 0:HD], o3,
                                               srg[:].rearrange("p (h d) -> p h d", d=HD), ALU.mult))

                    att_max(0)
                    dve.wait_ge(s_oret, t + 1)
                    dve.tensor_copy(osb[:], psO[0][:, 0:HW]).then_inc(s_oread, 1)
                    kv = psO[1][:].rearrange("p (g c) -> p g c", c=P)
                    for par in range(2):
                        e = slice(par * HD, par * HD + HD)
                        step(dve.tensor_tensor(state[e, :, e], state[e, :, e],
                                               cdecay[e, :].unsqueeze(2).to_broadcast([HD, G, HD]), ALU.mult))
                        dve.tensor_tensor(state[e, :, e], state[e, :, e], kv[e, :, e], ALU.add).then_inc(s_state, 1)
                    att_max(1)
                    for h in range(H):
                        att_weigh(h)
                        if h + 2 < H:
                            att_max(h + 2)
                        if h == 0:
                            groupnorm()
                        if h == 2:
                            gate()
                        if h == H - 4:
                            x_variance(t + 1)
                        if h == H - 3:
                            x_scale(t * 4 + 4)
                    dve.wait_ge(s_pv, t * H + H)
                    for n in range(2):
                        o = psO[n][:, 0:4 * VA].rearrange("p (h e) -> p h e", e=VA)
                        rd = rden[:, 4 * n:4 * n + 4]
                        step(dve.reciprocal(rd.unsqueeze(2), o[:, :, HD:VA]))
                        dve.tensor_tensor(mix[:].rearrange("p (h c) -> p h c", h=H)[:, 4 * n:4 * n + 4, HD:2 * HD],
                                          o[:, :, 0:HD], rd.unsqueeze(2).to_broadcast([P, 4, HD]), ALU.mult)\
                           .then_inc(s_mix, 1)
                    dve.wait_ge(s_xres, t * 16 + 16)
                    for half in range(2):
                        c = slice(half * 512, half * 512 + 512)
                        dve.wait_ge(s_wo, t * 2 + half + 2)
                        step(dve.tensor_tensor(xm[:, c], psS[0][:, c], gt1row[:, c], ALU.mult))
                        dve.tensor_tensor(xm[:, c], xm[:, c], xres[:, c], ALU.add).then_inc(s_xm, 1)
                    dve.wait_ge(s_xm, t * 2 + 3)
                    step(dve.tensor_tensor_reduce(junk[:], xm[:], xm[:], 1.0, 0.0, ALU.mult, ALU.add, ss))
                    dve.tensor_scalar(var, ss, 1.0 / D, EPS, ALU.mult, ALU.add).then_inc(s_var, 1)
                    dve.wait_ge(s_std, t * 4 + 5)
                    step(dve.reciprocal(rstd, std))
                    step(dve.scalar_tensor_tensor(out=h2[:], in0=xm[:], scalar=rstd, in1=a2row[:],
                                                  op0=ALU.mult, op1=ALU.mult))
                    dve.tensor_tensor(h2[:], h2[:], b2row[:], ALU.add).then_inc(s_h2, 1)

        @block.tensor
        def _(pe):
            for begun in (s_xm, s_state):
                pe.sem_inc(begun, 1)
            def turn_ada(c):
                pe.wait_ge(s_arow, c + 1)
                for m in range(4):
                    col = (c * 4 + m) * NC9
                    last = pe.transpose(psO[1][:, col:col + NC9], arow[c % 2][0:NC9, m * P:(m + 1) * P],
                                        ident[0:NC9, 0:NC9])
                last.then_inc(s_adaT, 1)

            pe.wait_ge(s_silu, 1)
            pe.wait_ge(s_ident, 16)
            for c in range(ADA_CHUNKS):
                pe.wait_ge(s_ada[c % WBUF], 16 * (c // WBUF + 1))
                if c >= 2:
                    pe.wait_ge(s_arow, c - 1)
                for k in range(KT):
                    last = pe.matmul(ps[c % 2][0:NC9, :], cT[:, k, :], w[c % WBUF][:, k, :],
                                     start=(k == 0), stop=(k == KT - 1))
                last.then_inc(s_adamm, 1)
                if c >= 1:
                    turn_ada(c - 1)
            turn_ada(ADA_CHUNKS - 1)

            def turn_x(n):
                pe.wait_ge(s_xn, n + 1)
                for half in range(2):
                    for j in range(4):
                        k = half * 4 + j
                        last = pe.transpose(psS[1][:, k * P:(k + 1) * P], xn[:, k * P:(k + 1) * P], ident[:])
                    last.then_inc(s_xT, 1)

            turn_x(0)
            pe.wait_ge(s_init, 4)
            for n in range(4):
                pe.wait_ge(s_diag, n + 1)
                if n == 1:
                    pe.wait_ge(s_hT, 2)
                if n >= 2:
                    pe.wait_ge(s_row, n - 1)
                for half in range(2):
                    c = slice(half * 512, half * 512 + 512)
                    last = pe.matmul(psS[n % 2][:, c], ones[:], diagonals[n][:, c], start=True, stop=True)
                last.then_inc(s_bc, 1)
            pe.wait_ge(s_row, 4)
            for first in range(0, T, SEG):
                keys = (first + SEG) * P
                with pe.Fori(first, first + SEG) as t:
                    def turn(src, n):
                        if n >= 2:
                            pe.wait_ge(s_te, t * 4 + n - 1)
                        for g in range(G):
                            last = pe.transpose(ps[n % 2][:, g * P:(g + 1) * P], src[:, g * P:(g + 1) * P], ident[:])
                        last.then_inc(s_tr, 1)

                    pe.wait_ge(s_hT, t * 2 + 2)
                    for c in range(NPROJ):
                        pe.wait_ge(s_w[c % WBUF], t * 16 * nbuf + 16 * (c // WBUF + 1))
                        if c == 2:
                            pe.wait_ge(s_xm, t * 2 + 1)
                        if c == 4:
                            pe.wait_ge(s_evD, t * 2 + 1)
                        if c == 5:
                            pe.wait_ge(s_evD, t * 2 + 2)
                        if c == 6:
                            pe.wait_ge(s_evA, t * 5 + 2)
                        bank = psS[1 - (c // 2) % 2][:, (c % 2) * 512:(c % 2) * 512 + 512]
                        for k in range(KT):
                            last = pe.matmul(bank, hT[:, k, :], w[c % WBUF][:, k, :], start=(k == 0), stop=(k == KT - 1))
                        last.then_inc(s_proj, 1)
                        if c == 4:
                            pe.wait_ge(s_evA, t * 5 + 2)
                            turn(rq, 0)
                        if c == 5:
                            pe.wait_ge(s_evA, t * 5 + 3)
                            turn(rk, 1)
                    pe.wait_ge(s_qkn, t + 1)
                    turn(qkn, 2)
                    turn(qkn[:, HW:2 * HW], 3)
                    pe.wait_ge(s_te, t * 4 + 2)
                    pe.wait_ge(s_evA, t * 5 + 5)
                    for par in range(2):
                        e = slice(par * HD, par * HD + HD)
                        for g in range(G):
                            c = (par * G + g) * P
                            last = pe.matmul(psS[1][:, c:c + P], rkT[e, g, :], rqT[e, g, :], start=True, stop=True)
                        last.then_inc(s_rs, 1)
                    pe.wait_ge(s_kw, t + 1)
                    pe.wait_ge(s_state, t * 2 + 1)
                    for g in range(G):
                        c = slice(g * P, g * P + P)
                        pe.matmul(psO[1][:, c], kw[:, c], rv[:, c], start=True, stop=True)
                    def scores(h):
                        e = slice((h % 2) * HD, (h % 2) * HD + HD)
                        if h >= 2:
                            pe.wait_ge(s_nm, t * H + h - 1)
                        for c in halves(keys):
                            last = pe.matmul(psS[h % 2][:, c], aqT[e, h // 2, :], kT[e, h // 2, c], start=True, stop=True)
                        last.then_inc(s_S, 1)

                    pe.wait_ge(s_te, t * 4 + 4)
                    pe.wait_ge(s_evA, t * 5 + 6)
                    scores(0)
                    pe.wait_ge(s_qTw, t + 1)
                    pe.wait_ge(s_sT, t * 2 + 2)
                    for g in range(G):
                        pe.matmul(psO[0][:, g * P:(g + 1) * P], qTw[:, g, :], state[:, g, :], start=True, stop=False)
                        for par in range(2):
                            c, o = (par * G + g) * P, (2 * g + par) * HD
                            last = pe.matmul(psO[0][:, o:o + HD], sT[:, c:c + P], rv[:, o:o + HD],
                                             start=False, stop=(par == 1))
                    last.then_inc(s_oret, 1)

                    scores(1)
                    for h in range(H):
                        pe.wait_ge(s_P, t * H + h + 1)
                        for half, c in enumerate(halves(keys)):
                            if h >= 1:
                                pe.wait_ge(s_PT, t * 2 * H + 2 * (h - 1) + half + 1)
                            for k in range(c.start // P, c.stop // P):
                                j = k - half * 4
                                last = pe.transpose(ps[half][:, j * P:(j + 1) * P],
                                                    sp[h % 2][:, k * P:(k + 1) * P], ident[:])
                            last.then_inc(s_pt, 2 // len(halves(keys)))
                        if h + 2 < H:
                            scores(h + 2)
                        if h == H - 1:
                            turn_x(t + 1)
                        if h == 0:
                            pe.wait_ge(s_vaug, t + 1)
                            pe.wait_ge(s_oread, t + 1)
                            pe.wait_ge(s_state, t * 2 + 3)
                        pe.wait_ge(s_PT, t * 2 * H + 2 * h + 2)
                        for k in range(keys // P):
                            last = pe.matmul(psO[h // 4][:, (h % 4) * VA:(h % 4) * VA + VA], pt[h % 2][:, k * P:(k + 1) * P],
                                             va[:, k, h * VA:(h + 1) * VA], start=(k == 0), stop=(k == keys // P - 1))
                        last.then_inc(s_pv, 1)
                    pe.wait_ge(s_mix, t * 2 + 2)
                    for half in range(2):
                        for j in range(4):
                            k = half * 4 + j
                            last = pe.transpose(ps[half][:, j * P:(j + 1) * P], mix[:, k * P:(k + 1) * P], ident[:])
                        last.then_inc(s_mT, 1)
                    pe.wait_ge(s_mixT, t * 2 + 2)
                    for c in range(NPROJ, CHUNKS):
                        pe.wait_ge(s_w[c % WBUF], t * 16 * nbuf + 16 * (c // WBUF + 1))
                        n = c - NPROJ
                        for k in range(KT):
                            last = pe.matmul(psS[0][:, n * 512:(n + 1) * 512], mixT[:, k, :], w[c % WBUF][:, k, :],
                                             start=(k == 0), stop=(k == KT - 1))
                        last.then_inc(s_wo, 1)


def decode(nc, a, sem, ps, psS, psO, ident, tabs):
    BH = B * H
    LOTS = 4
    with ExitStack() as ctx:
        def sb(name, shape, dt=F32):
            return ctx.enter_context(nc.sbuf_tensor("de_" + name, shape, dt))

        w = [sb(f"w{i}", [P, KT, 512]) for i in range(WBUF)]
        xs = sb("xs", [B, D])
        xns = sb("xns", [B, D])
        junk = sb("junk", [B, D])
        xms = sb("xms", [B, D])
        h2s = sb("h2s", [B, D])
        rows = sb("rows", [B, 4, D])
        hTs = sb("hTs", [P, KT, B])
        mixs = sb("mixs", [B, D])
        mixTs = sb("mixTs", [P, KT, B])
        proj = sb("proj", [B, NPROJ, HW])
        pj = sb("pj", [BH, NPROJ, HD])
        gqk = sb("gqk", [BH, 2, HD])
        gret = sb("gret", [BH, HD])
        gamma = sb("gamma", [BH, 1])
        bias = sb("bias", [BH, NSEL + 1])
        count = sb("count", [BH, NSEL + 1])
        s0 = sb("s0", [BH, HD, HD])
        prod = sb("prod", [BH, HD, HD])
        kv = [sb(f"kv{i}", [BH, HD * HD]) for i in range(2)]
        sq = sb("sq", [BH, 2, HD])
        o = sb("o", [BH, HD])
        osum = sb("osum", [BH, HD])
        part = sb("part", [BH, HD])
        srg = sb("srg", [BH, HD])
        mix = sb("mix", [BH, 2, HD])
        S = sb("S", [BH, NSEL + 1])
        st = sb("st", [BH, 16])
        stB = sb("stB", [B, 4])
        zeros = sb("zeros", [P, D])

        s_ld = sem("sample_loaded")
        s_w = [sem(f"sample_weight{i}") for i in range(WBUF)]
        s_kv = [sem(f"sample_cache{i}") for i in range(2)]
        s_kvu = sem("sample_cache_used")
        s_var = sem("sample_variance")
        s_std = sem("sample_deviation")
        s_xn = sem("sample_normed")
        s_tr = sem("sample_turned_psum")
        s_hT = sem("sample_turned_copied")
        s_rows = sem("sample_rows_psum")
        s_rowc = sem("sample_rows_copied")
        s_proj = sem("sample_projected")
        s_pc = sem("sample_projection_copied")
        s_pst = sem("sample_projection_stored")
        s_pj = sem("sample_heads_loaded")
        s_akn = sem("sample_keys_normed")
        s_silu = sem("sample_silu")
        s_state = sem("sample_state")
        s_max = sem("sample_max")
        s_exp = sem("sample_exp")
        s_mix = sem("sample_mixed")
        s_mst = sem("sample_mix_stored")
        s_mld = sem("sample_mix_loaded")
        s_mT = sem("sample_mix_turned")
        s_mTc = sem("sample_mix_turned_copied")
        s_wo = sem("sample_out_projected")
        s_h2 = sem("sample_h2")
        s_z = sem("sample_zeros")
        s_st = sem("sample_stored")
        s_ch = sem("sample_dve_step")

        w_in = a["w_in"].rearrange("(k p) n -> p k n", p=P)
        w_out = a["w_out"].rearrange("(k p) n -> p k n", p=P)
        smalls = [(xs, "x_sample"), (gqk, "g_qk_s"), (gret, "g_ret_s"), (gamma, "c_gamma"), (bias, "c_bias_s"),
                  (count, "c_count_s"), (s0, "state_s")]
        STORES = 6
        block = ctx.enter_context(nc.Block())

        @block.sync
        def _(sp):
            for tile, name in smalls:
                sp.dma_start(tile[:], a[name]).then_inc(s_ld, 16)
            for c in range(CHUNKS):
                if c >= WBUF:
                    sp.wait_ge(s_proj, c - WBUF + 1)
                src = (w_in[:, :, c * HW:(c + 1) * HW] if c < NPROJ
                       else w_out[:, :, (c - NPROJ) * 512:(c - NPROJ + 1) * 512])
                sp.dma_start(w[c % WBUF][:], src).then_inc(s_w[c % WBUF], 16)
            for n in range(2 * LOTS):
                if n >= 2:
                    sp.wait_ge(s_kvu, n - 1)
                src = a["k_sel" if n < LOTS else "v_sel"][:, ds((n % LOTS) * HD * HD, HD * HD)]
                sp.dma_start(kv[n % 2][:], src).then_inc(s_kv[n % 2], 16)

        @block.gpsimd
        def _(pool):
            pool.memset(zeros[:], 0.0).then_inc(s_z, 1)
            pool.wait_ge(s_z, 1)
            pool.dma_start(a["h2"][T * P + B:(T + 1) * P, :], zeros[0:P - B, :]).then_inc(s_st, 16)
            pool.wait_ge(s_pc, NPROJ)
            pool.dma_start(a["proj_s"].rearrange("s b n -> b s n"), proj[:]).then_inc(s_pst, 16)
            pool.wait_ge(s_pst, 16)
            pool.dma_start(pj[:], a["proj_s"].rearrange("s b (h d) -> (b h) s d", d=HD)).then_inc(s_pj, 16)
            pool.wait_ge(s_pj, 16)
            pool.dma_start(a["wv_sample"], pj[:, 6, :]).then_inc(s_st, 16)
            pool.wait_ge(s_akn, 1)
            pool.dma_start(a["wk_sample"], pj[:, 5, :]).then_inc(s_st, 16)
            pool.wait_ge(s_state, 1)
            pool.dma_start(a["ret_sample"], s0[:].rearrange("p d e -> p (d e)")).then_inc(s_st, 16)
            pool.wait_ge(s_mix, 1)
            pool.dma_start(a["mix_s"], mix[:].rearrange("p c d -> p (c d)")).then_inc(s_mst, 16)
            pool.wait_ge(s_mst, 16)
            pool.dma_start(mixs[:], a["mix_s"].rearrange("(b h) c -> b (h c)", b=B)).then_inc(s_mld, 16)
            pool.wait_ge(s_rowc, 4)
            pool.dma_start(a["gt2_sample"], rows[:, 3, :]).then_inc(s_st, 16)
            pool.wait_ge(s_h2, 2)
            pool.dma_start(a["x_mid"][T * P:T * P + B, :], xms[:]).then_inc(s_st, 16)
            pool.dma_start(a["h2"][T * P:T * P + B, :], h2s[:]).then_inc(s_st, 16)
            pool.wait_ge(s_st, 16 * (STORES + 1))

        @block.scalar
        def _(act):
            for n in range(4):
                act.wait_ge(s_rows, n + 1)
                act.activation(rows[:, n, :], psS[n % 2][0:B, :], ACT.Copy).then_inc(s_rowc, 1)
            act.wait_ge(s_var, 1)
            act.activation(stB[:, 2:3], stB[:, 1:2], ACT.Sqrt).then_inc(s_std, 1)
            for c in range(NPROJ):
                act.wait_ge(s_proj, c + 1)
                act.activation(proj[:, c, :], ps[c % 2][0:B, :], ACT.Copy).then_inc(s_pc, 1)
            act.wait_ge(s_pj, 16)
            act.activation(srg[:], pj[:, 3, :], ACT.Silu).then_inc(s_silu, 1)
            act.wait_ge(s_var, 2)
            act.activation(st[:, 4:6], st[:, 2:4], ACT.Sqrt).then_inc(s_std, 1)
            act.wait_ge(s_var, 3)
            act.activation(st[:, 9:10], st[:, 8:9], ACT.Sqrt).then_inc(s_std, 1)
            act.wait_ge(s_max, 1)
            act.activation(S[:], S[:], ACT.Exp, bias=st[:, 11:12]).then_inc(s_exp, 1)
            act.wait_ge(s_var, 4)
            act.activation(stB[:, 2:3], stB[:, 1:2], ACT.Sqrt).then_inc(s_std, 1)

        @block.tensor
        def _(pe):
            for n, sec_no in enumerate((2, 3, 4, 5)):
                if n >= 2:
                    pe.wait_ge(s_rowc, n - 1)
                for k in range(KT):
                    last = pe.transpose(psS[n % 2][0:B, k * P:(k + 1) * P], tabs[:, sec_no, k, 0:B], ident[:])
                last.then_inc(s_rows, 1)
            pe.wait_ge(s_xn, 1)
            for k in range(KT):
                last = pe.transpose(psO[0][:, k * B:(k + 1) * B], xns[:, k * P:(k + 1) * P], ident[0:B, 0:B])
            last.then_inc(s_tr, 1)
            pe.wait_ge(s_hT, 1)
            for c in range(NPROJ):
                pe.wait_ge(s_w[c % WBUF], 16 * (c // WBUF + 1))
                if c >= 2:
                    pe.wait_ge(s_pc, c - 1)
                for k in range(KT):
                    last = pe.matmul(ps[c % 2][0:B, :], hTs[:, k, :], w[c % WBUF][:, k, :],
                                     start=(k == 0), stop=(k == KT - 1))
                last.then_inc(s_proj, 1)
            pe.wait_ge(s_mld, 16)
            for k in range(KT):
                last = pe.transpose(psO[1][:, k * B:(k + 1) * B], mixs[:, k * P:(k + 1) * P], ident[0:B, 0:B])
            last.then_inc(s_mT, 1)
            pe.wait_ge(s_mTc, 1)
            pe.wait_ge(s_rowc, 4)
            for c in range(NPROJ, CHUNKS):
                pe.wait_ge(s_w[c % WBUF], 16 * (c // WBUF + 1))
                n = c - NPROJ
                for k in range(KT):
                    last = pe.matmul(psS[0][0:B, n * 512:(n + 1) * 512], mixTs[:, k, :], w[c % WBUF][:, k, :],
                                     start=(k == 0), stop=(k == KT - 1))
                last.then_inc(s_wo, 1)

        @block.vector
        def _(dve):
            steps = [0]

            def step(ins):
                steps[0] += 1
                ins.then_inc(s_ch, 1)
                dve.wait_ge(s_ch, steps[0])

            def norm(src, n):
                step(dve.tensor_tensor_reduce(junk[:], src[:], src[:], 1.0, 0.0, ALU.mult, ALU.add, stB[:, 0:1]))
                dve.tensor_scalar(stB[:, 1:2], stB[:, 0:1], 1.0 / D, EPS, ALU.mult, ALU.add).then_inc(s_var, 1)
                dve.wait_ge(s_std, n)
                step(dve.reciprocal(stB[:, 3:4], stB[:, 2:3]))

            dve.wait_ge(s_ld, 16 * len(smalls))
            norm(xs, 1)
            dve.tensor_scalar(xns[:], xs[:], stB[:, 3:4], None, ALU.mult).then_inc(s_xn, 1)
            dve.wait_ge(s_tr, 1)
            step(dve.tensor_tensor(hTs[:], psO[0][:, 0:KT * B].rearrange("p (k b) -> p k b", b=B),
                                   tabs[:, 0, :, 0:B], ALU.mult))
            dve.tensor_tensor(hTs[:], hTs[:], tabs[:, 1, :, 0:B], ALU.add).then_inc(s_hT, 1)
            dve.wait_ge(s_pj, 16)
            qk = pj[:, 4:6, :]
            step(dve.tensor_tensor(sq[:], qk, qk, ALU.mult))
            step(dve.tensor_reduce(st[:, 0:2], sq[:], AX, ALU.add))
            dve.tensor_scalar(st[:, 2:4], st[:, 0:2], 1.0 / HD, EPS, ALU.mult, ALU.add).then_inc(s_var, 1)
            dve.wait_ge(s_std, 2)
            step(dve.reciprocal(st[:, 6:8], st[:, 4:6]))
            step(dve.tensor_tensor(qk, qk, st[:, 6:8].unsqueeze(2).to_broadcast([BH, 2, HD]), ALU.mult))
            dve.tensor_tensor(qk, qk, gqk[:], ALU.mult).then_inc(s_akn, 1)
            dve.wait_ge(s_akn, 1)
            rq, rk, rv, aq, ak, av = (pj[:, i, :] for i in (0, 1, 2, 4, 5, 6))
            step(dve.tensor_scalar(rk, rk, HD ** -0.5, None, ALU.mult))
            step(dve.tensor_scalar(aq, aq, HD ** -0.5, None, ALU.mult))
            step(dve.tensor_tensor(prod[:], s0[:], rq.unsqueeze(2).to_broadcast([BH, HD, HD]), ALU.mult))
            step(dve.tensor_reduce(o[:], prod[:].rearrange("p d e -> p e d"), AX, ALU.add))
            step(dve.tensor_tensor_reduce(sq[:, 0, :], rq, rk, 1.0, 0.0, ALU.mult, ALU.add, st[:, 12:13]))
            step(dve.tensor_scalar(sq[:, 1, :], rv, st[:, 12:13], None, ALU.mult))
            step(dve.scalar_tensor_tensor(out=o[:], in0=o[:], scalar=gamma[:], in1=sq[:, 1, :],
                                          op0=ALU.mult, op1=ALU.add))
            step(dve.tensor_tensor(prod[:], rk.unsqueeze(2).to_broadcast([BH, HD, HD]),
                                   rv.unsqueeze(1).to_broadcast([BH, HD, HD]), ALU.mult))
            dve.scalar_tensor_tensor(out=s0[:], in0=s0[:], scalar=gamma[:], in1=prod[:],
                                     op0=ALU.mult, op1=ALU.add).then_inc(s_state, 1)
            step(dve.tensor_reduce(st[:, 13:14], o[:], AX, ALU.add))
            step(dve.tensor_scalar(st[:, 13:14], st[:, 13:14], -1.0 / HD, None, ALU.mult))
            step(dve.tensor_scalar(o[:], o[:], st[:, 13:14], None, ALU.add))
            step(dve.tensor_tensor_reduce(sq[:, 0, :], o[:], o[:], 1.0, 0.0, ALU.mult, ALU.add, st[:, 14:15]))
            dve.tensor_scalar(st[:, 8:9], st[:, 14:15], 1.0 / HD, EPS, ALU.mult, ALU.add).then_inc(s_var, 1)
            dve.wait_ge(s_std, 3)
            step(dve.reciprocal(st[:, 10:11], st[:, 9:10]))
            step(dve.scalar_tensor_tensor(out=o[:], in0=o[:], scalar=st[:, 10:11], in1=gret[:],
                                          op0=ALU.mult, op1=ALU.mult))
            dve.wait_ge(s_silu, 1)
            step(dve.tensor_tensor(mix[:, 0, :], o[:], srg[:], ALU.mult))
            J = NSEL // LOTS
            for n in range(LOTS):
                dve.wait_ge(s_kv[n % 2], 16 * (n // 2 + 1))
                kk = kv[n % 2][:].rearrange("p (j d) -> p j d", d=HD)
                step(dve.tensor_tensor(kk, kk, aq.unsqueeze(1).to_broadcast([BH, J, HD]), ALU.mult))
                dve.tensor_reduce(S[:, n * J:(n + 1) * J], kk, AX, ALU.add).then_inc(s_kvu, 1)
            dve.wait_ge(s_kvu, LOTS)
            step(dve.tensor_tensor_reduce(sq[:, 0, :], aq, ak, 1.0, 0.0, ALU.mult, ALU.add, S[:, NSEL:NSEL + 1]))
            step(dve.tensor_tensor_reduce(S[:], S[:], bias[:], 1.0, LOWEST, ALU.add, ALU.max, st[:, 15:16]))
            dve.tensor_scalar(st[:, 11:12], st[:, 15:16], -1.0, None, ALU.mult).then_inc(s_max, 1)
            dve.wait_ge(s_exp, 1)
            step(dve.tensor_tensor_reduce(S[:], S[:], count[:], 1.0, 0.0, ALU.mult, ALU.add, st[:, 0:1]))
            step(dve.reciprocal(st[:, 1:2], st[:, 0:1]))
            for n in range(LOTS):
                m, E = n + LOTS, HD // LOTS
                dve.wait_ge(s_kv[m % 2], 16 * (m // 2 + 1))
                vv = kv[m % 2][:].rearrange("p (e j) -> p e j", j=NSEL)
                step(dve.tensor_tensor(vv, vv, S[:, 0:NSEL].unsqueeze(1).to_broadcast([BH, E, NSEL]), ALU.mult))
                dve.tensor_reduce(osum[:, n * E:(n + 1) * E], vv, AX, ALU.add).then_inc(s_kvu, 1)
            dve.wait_ge(s_kvu, 2 * LOTS)
            step(dve.scalar_tensor_tensor(out=osum[:], in0=av, scalar=S[:, NSEL:NSEL + 1], in1=osum[:],
                                          op0=ALU.mult, op1=ALU.add))
            dve.tensor_scalar(mix[:, 1, :], osum[:], st[:, 1:2], None, ALU.mult).then_inc(s_mix, 1)
            dve.wait_ge(s_mT, 1)
            dve.tensor_copy(mixTs[:], psO[1][:, 0:KT * B].rearrange("p (k b) -> p k b", b=B)).then_inc(s_mTc, 1)
            dve.wait_ge(s_wo, 2)
            step(dve.tensor_tensor(xms[:], psS[0][0:B, :], rows[:, 0, :], ALU.mult))
            dve.tensor_tensor(xms[:], xms[:], xs[:], ALU.add).then_inc(s_h2, 1)
            dve.wait_ge(s_h2, 1)
            norm(xms, 4)
            step(dve.scalar_tensor_tensor(out=h2s[:], in0=xms[:], scalar=stB[:, 3:4], in1=rows[:, 1, :],
                                          op0=ALU.mult, op1=ALU.mult))
            dve.tensor_tensor(h2s[:], h2s[:], rows[:, 2, :], ALU.add).then_inc(s_h2, 1)


def peer(nc, a, sem, ps, psS, psO, ident, gt2row):
    AHEAD = 4
    ROWS_S = HP * B
    with ExitStack() as ctx:
        def sb(name, shape, dt=F32):
            return ctx.enter_context(nc.sbuf_tensor("pr_" + name, shape, dt))

        wpq = sb("wpq", [P, KT, HP * P])
        subk = sb("subk", [P, HP, 2 * NK])
        iota = sb("iota", [P, TOPK])
        spread = sb("spread", [B, B, P])
        ring = [sb(f"ring{i}", [P, 2 * D]) for i in range(RING)]
        h2cur = sb("h2cur", [P, D])
        h2next = sb("h2next", [P, D])
        h2T = sb("h2T", [P, KT, P])
        xmid = sb("xmid", [P, D])
        ysum = sb("ysum", [P, D])
        diag = sb("diag", [P, TOPK, P])
        zeros = sb("zeros", [P, P])
        qh = sb("qh", [P, P])
        qhT = sb("qhT", [P, P])
        sc = [sb(f"sc{u}", [P, 2 * NK]) for u in range(2)]
        work = sb("work", [P, 256])
        cand = sb("cand", [P, TOPK, TOPK])
        top = sb("top", [P, 3, TOPK])
        pos = sb("pos", [P, 3, TOPK], U32)
        half_pos = sb("half_pos", [P, 2, TOPK], U32)
        half_f = sb("half_f", [P, 2, TOPK])
        key_f = sb("key_f", [P, 2, TOPK])
        hit = sb("hit", [P, TOPK, TOPK])
        pick = sb("pick", [P, 2, TOPK])
        expert_f = [sb(f"expert_f{u}", [P, TOPK]) for u in range(2)]
        expert = [sb(f"expert{u}", [P, TOPK], U32) for u in range(2)]
        delta = [sb(f"delta{u}", [P, TOPK]) for u in range(2)]
        gate_h = [sb(f"gate_h{u}", [P, TOPK]) for u in range(2)]
        gsum = [sb(f"gsum{u}", [P, 2]) for u in range(2)]
        dot = sb("dot", [P, TOPK])
        act_h = sb("act_h", [P, TOPK])
        h2s = sb("h2s", [B, D])
        h2sT = sb("h2sT", [P, KT, B])
        q_s = sb("q_s", [B, D])
        qT_s = sb("qT_s", [P, HP * (ROWS_S + B)])
        sc_s = sb("sc_s", [ROWS_S, 2 * NK])
        expert_s = sb("expert_s", [ROWS_S, TOPK])
        delta_s = sb("delta_s", [ROWS_S, TOPK])
        gate_s = sb("gate_s", [ROWS_S, TOPK])
        gsum_s = sb("gsum_s", [ROWS_S, 2])
        expT_f = sb("expT_f", [P, B])
        expT = sb("expT", [P, B], U32)
        gateT = sb("gateT", [P, B])
        coef = sb("coef", [P, B, B])
        gt2s = sb("gt2s", [B, D])
        xmid_s = sb("xmid_s", [B, D])
        y_s = sb("y_s", [B, D])

        s_w = sem("peer_weights")
        s_ws = sem("peer_sample_inputs")
        s_set = sem("peer_buffers_set")
        s_h2 = sem("h2_loaded")
        s_cur = sem("h2_current")
        s_hT = sem("h2_turned")
        s_hTc = sem("h2_turned_copied")
        s_qh = sem("peer_query")
        s_qhc = sem("peer_query_copied")
        s_qT = sem("peer_query_turned")
        s_qTc = sem("peer_query_turned_copied")
        s_sc = sem("peer_scores")
        s_scc = sem("peer_scores_copied")
        s_scu = sem("peer_scores_used")
        s_top = sem("experts_chosen")
        s_g = [sem(f"gathered{i}") for i in range(RING)]
        s_ge = sem("gates_exp")
        s_dot = sem("dots")
        s_gelu = sem("gelu")
        s_coef = sem("expert_weights")
        s_dg = sem("diagonals")
        s_free = sem("ring_free")
        s_y = sem("peer_summed")
        s_yc = sem("peer_sum_copied")
        s_xm = sem("x_mid_loaded")
        s_out = sem("y_ready")
        s_st = sem("y_stored")
        s_ch = sem("dve_peer_step")
        s_passed = sem("peer_wait_passed")
        s_sp = sem("sample_turns")
        s_sa = sem("sample_turns_copied")
        s_tops = sem("sample_experts_chosen")
        s_ges = sem("sample_gates_exp")
        s_gts = sem("sample_gates")
        s_xs = sem("sample_experts_stored")
        s_xl = sem("sample_experts_loaded")
        s_xT = sem("sample_experts_placed")
        s_bc = sem("sample_h2_spread")
        s_ys = sem("y_sample_stored")

        GROUPS = TOPK // GRP
        N = T * HP
        PAIRS = HP // 2
        assert AHEAD == HP // 2 and PAIRS % 2 == 0
        block = ctx.enter_context(nc.Block())

        @block.sync
        def _(sp):
            for begun in (s_out, s_st):
                sp.sem_inc(begun, 1)
            sp.dma_start(h2next[:], a["h2"][0:P, :]).then_inc(s_h2, 16)
            sp.dma_start(wpq[:], a["w_pq"].rearrange("(k p) n -> p k n", p=P)).then_inc(s_w, 16)
            sp.dma_start(subk[:], a["subk"]).then_inc(s_w, 16)
            sp.dma_start(iota[:], a["c_iota"]).then_inc(s_w, 16)
            sp.dma_start(h2s[:], a["h2"][T * P:T * P + B, :]).then_inc(s_ws, 16)
            sp.dma_start(gt2s[:], a["gt2_sample"]).then_inc(s_ws, 16)
            sp.dma_start(xmid_s[:], a["x_mid"][T * P:T * P + B, :]).then_inc(s_ws, 16)
            sp.dma_start(spread[:], a["c_spread"]).then_inc(s_ws, 16)
            for n, (src, name) in enumerate(((expert_s, "expert_s"), (gate_s, "gate_s"))):
                sp.wait_ge(s_gts, n + 1)
                sp.dma_start(a[name].rearrange("h b k -> (h b) k"), src[:]).then_inc(s_xs, 16)
            sp.wait_ge(s_xs, 32)
            for dst, name in ((expT_f, "expert_s"), (gateT, "gate_s")):
                for h in range(HP):
                    sp.dma_start(dst[h * TOPK:(h + 1) * TOPK, :], a[name][h].rearrange("b k -> k b"),
                                 allow_slow_non_contiguous=True).then_inc(s_xl, 16)
            with sp.Fori(0, T) as t:
                sp.wait_ge(s_cur, t + 1)
                sp.dma_start(h2next[:], a["h2"][ds((t + 1) * P, P), :]).then_inc(s_h2, 16)
                sp.wait_ge(s_out, t + 1)
                sp.dma_start(xmid[:], a["x_mid"][ds(t * P, P), :]).then_inc(s_xm, 16)
                sp.wait_ge(s_out, t + 2)
                sp.dma_start(a["y_prompt"][ds(t * P, P), :], ysum[:]).then_inc(s_st, 16)
            sp.wait_ge(s_out, T + 2)
            sp.dma_start(a["y_sample"], y_s[:]).then_inc(s_ys, 16)
            sp.wait_ge(s_ys, 16)
            sp.wait_ge(s_st, 16 * T + 1)

        @block.gpsimd
        def _(pool):
            def gather(r, index):
                pool.indirect_dma_start(ring[r][:], None, a["uv"],
                                        bass.IndirectOffsetOnAxis(ap=index, axis=0)).then_inc(s_g[r], 16)

            with pool.Fori(0, N // 2) as pair:
                for u in range(2):
                    n = pair * 2 + u
                    pool.wait_ge(s_top, n + 1)
                    for s in range(TOPK):
                        if s % GRP == 0:
                            pool.wait_ge(s_free, n * GROUPS + s // GRP + 1)
                            pool.sem_inc(s_passed, 1)
                        gather(s % RING, expert[u][:, s:s + 1])
            pool.wait_ge(s_xl, 32 * HP)
            pool.tensor_copy(expT[:], expT_f[:]).then_inc(s_xT, 1)
            pool.wait_ge(s_xT, 1)
            for b in range(B):
                if b % GRP == 0:
                    pool.wait_ge(s_free, N * GROUPS + b // GRP + 1)
                gather(b, expT[:, b:b + 1])

        @block.scalar
        def _(act):
            def turned():
                for half in range(2):
                    act.activation(h2T[:, half * 4:half * 4 + 4, :],
                                   psS[1][:, half * 512:half * 512 + 512].rearrange("p (g i) -> p g i", g=4),
                                   ACT.Copy).then_inc(s_hTc, 1)

            def query_out(n):
                act.wait_ge(s_qh, n + 1)
                act.activation(qh[:], ps[0][:, 0:P], ACT.Copy).then_inc(s_qhc, 1)

            def turned_query_out(n):
                act.wait_ge(s_qT, n + 1)
                act.activation(qhT[:], ps[1][:, 0:P], ACT.Copy).then_inc(s_qTc, 1)

            def scores_out(n, u):
                act.wait_ge(s_sc, n + 1)
                act.activation(sc[u][:], psO[0][:, 0:2 * NK], ACT.Copy).then_inc(s_scc, 1)

            act.wait_ge(s_hT, 2)
            turned()
            for n in range(AHEAD):
                query_out(n)
                turned_query_out(n)
                if n >= 2:
                    act.wait_ge(s_scu, n - 1)
                scores_out(n, n % 2)
                if n == 1:
                    act.wait_ge(s_sp, 1)
                    act.activation(h2sT[:], psO[1][:, 0:KT * B].rearrange("p (k b) -> p k b", b=B), ACT.Copy)\
                       .then_inc(s_sa, 1)
                    act.wait_ge(s_sp, 2)
                    act.activation(q_s[:], psS[1][0:B, :], ACT.Copy).then_inc(s_sa, 1)
                    act.wait_ge(s_sp, 3)
                    act.wait_ge(s_set, 3)
                    act.activation(qT_s[:].rearrange("p (h c) -> p h c", h=HP)[:, :, 0:B],
                                   psO[1][:, 0:HP * B].rearrange("p (h b) -> p h b", b=B), ACT.Copy).then_inc(s_sa, 1)
                    act.wait_ge(s_sp, 4)
                    act.activation(sc_s[:], psS[1][0:ROWS_S, 0:2 * NK], ACT.Copy).then_inc(s_sa, 1)
            act.wait_ge(s_tops, 1)
            act.activation(gate_s[:], delta_s[:], ACT.Exp, accum_out=gsum_s[:, 0:1]).then_inc(s_ges, 1)
            with act.Fori(0, T) as t:
                for half in range(2):
                    if half == 1:
                        act.wait_ge(s_hT, t * 2 + 4)
                        turned()
                    with act.Fori(half * PAIRS // 2, (half + 1) * PAIRS // 2) as pair:
                        for u in range(2):
                            n = t * HP + pair * 2 + u
                            act.wait_ge(s_top, n + 1)
                            act.activation(gate_h[u][:], delta[u][:], ACT.Exp, accum_out=gsum[u][:, 0:1])\
                               .then_inc(s_ge, 1)
                            for q in range(GROUPS):
                                act.wait_ge(s_dot, n * GROUPS + q + 1)
                                c = slice(q * GRP, q * GRP + GRP)
                                act.activation(act_h[:, c], dot[:, c], ACT.Gelu).then_inc(s_gelu, 1)
                                if q == 2:
                                    query_out(n + AHEAD)
                                if q == 4:
                                    turned_query_out(n + AHEAD)
                                if q == 6:
                                    act.wait_ge(s_scu, n + 3)
                                    scores_out(n + AHEAD, u)
                act.wait_ge(s_y, t + 1)
                act.wait_ge(s_st, t * 16 + 1)
                act.activation(ysum[:], psS[0][:], ACT.Copy).then_inc(s_yc, 1)
            for b in range(B):
                act.wait_ge(s_dot, N * GROUPS + b + 1)
                act.activation(act_h[:, b:b + 1], dot[:, b:b + 1], ACT.Gelu).then_inc(s_gelu, 1)

        @block.tensor
        def _(pe):
            for begun in (s_qhc, s_scc, s_yc):
                pe.sem_inc(begun, 1)

            def turn():
                for half in range(2):
                    for j in range(4):
                        k = half * 4 + j
                        last = pe.transpose(psS[1][:, k * P:(k + 1) * P], h2next[:, k * P:(k + 1) * P], ident[:])
                    last.then_inc(s_hT, 1)

            def query(h, n):
                pe.wait_ge(s_qhc, n + 1)
                for k in range(KT):
                    last = pe.matmul(ps[0][:, 0:P], h2T[:, k, :], wpq[:, k, ds(h * P, P)],
                                     start=(k == 0), stop=(k == KT - 1))
                last.then_inc(s_qh, 1)

            def turn_query(n):
                pe.wait_ge(s_qhc, n + 2)
                pe.transpose(ps[1][:, 0:P], qh[:], ident[:]).then_inc(s_qT, 1)

            def scores(h, n):
                pe.wait_ge(s_qTc, n + 1)
                pe.wait_ge(s_scc, n + 1)
                pe.matmul(psO[0][:, 0:2 * NK], qhT[:], subk[:, ds(h, 1), :].rearrange("p o k -> p (o k)"),
                          start=True, stop=True).then_inc(s_sc, 1)

            def spread_h2(b):
                for half in range(2):
                    c = slice(half * 512, half * 512 + 512)
                    last = pe.matmul(psS[1][:, c], spread[:, b, :], h2s[:, c], start=True, stop=True)
                last.then_inc(s_bc, 1)

            pe.wait_ge(s_h2, 16)
            turn()
            pe.wait_ge(s_w, 48)
            pe.wait_ge(s_hTc, 2)
            for n in range(AHEAD):
                query(n, n)
                turn_query(n)
                scores(n, n)
                if n == 1:
                    pe.wait_ge(s_ws, 64)
                    for k in range(KT):
                        last = pe.transpose(psO[1][:, k * B:(k + 1) * B], h2s[:, k * P:(k + 1) * P], ident[0:B, 0:B])
                    last.then_inc(s_sp, 1)
                    pe.wait_ge(s_sa, 1)
                    for half in range(2):
                        c = slice(half * 512, half * 512 + 512)
                        for k in range(KT):
                            last = pe.matmul(psS[1][0:B, c], h2sT[:, k, :], wpq[:, k, c],
                                             start=(k == 0), stop=(k == KT - 1))
                    last.then_inc(s_sp, 1)
                    pe.wait_ge(s_sa, 2)
                    for h in range(HP):
                        last = pe.transpose(psO[1][:, h * B:(h + 1) * B], q_s[:, h * P:(h + 1) * P], ident[0:B, 0:B])
                    last.then_inc(s_sp, 1)
                    pe.wait_ge(s_sa, 3)
                    for h in range(HP):
                        last = pe.matmul(psS[1][0:ROWS_S, 0:2 * NK], qT_s[:, h * ROWS_S:(h + 1) * ROWS_S],
                                         subk[:, h, :], start=(h == 0), stop=(h == HP - 1))
                    last.then_inc(s_sp, 1)
            pe.wait_ge(s_set, 3)
            pe.wait_ge(s_sa, 4)
            with pe.Fori(0, T) as t:
                pe.wait_ge(s_yc, t + 1)
                for half in range(2):
                    pe.matmul(psS[0][:, half * 512:half * 512 + 512], zeros[:], wpq[:, 0, 0:512],
                              start=True, stop=False, skip_group_check=True)
                for part in range(2):
                    if part == 1:
                        pe.wait_ge(s_h2, t * 16 + 32)
                        turn()
                        pe.wait_ge(s_hTc, t * 2 + 4)
                        pe.sem_inc(s_passed, 1)
                    with pe.Fori(part * PAIRS // 2, (part + 1) * PAIRS // 2) as pair:
                        for u in range(2):
                            n = t * HP + pair * 2 + u
                            head = pair * 2 + (u + AHEAD - part * HP)
                            for q in range(GROUPS):
                                pe.wait_ge(s_dg, n * GROUPS + q + 1)
                                for s in range(q * GRP, q * GRP + GRP):
                                    for half in range(2):
                                        c = slice(half * 512, half * 512 + 512)
                                        last = pe.matmul(psS[0][:, c], diag[:, s, :],
                                                         ring[s % RING][:, D + c.start:D + c.stop],
                                                         start=False, stop=False, skip_group_check=True)
                                last.then_inc(s_free, 1)
                                if q == 0:
                                    query(head, n + AHEAD)
                                if q == 2:
                                    turn_query(n + AHEAD)
                                if q == 4:
                                    scores(head, n + AHEAD)
                for half in range(2):
                    last = pe.matmul(psS[0][:, half * 512:half * 512 + 512], zeros[:], wpq[:, 0, 0:512],
                                     start=False, stop=True, skip_group_check=True)
                last.then_inc(s_y, 1)
            spread_h2(0)
            pe.wait_ge(s_yc, T + 1)
            for b in range(B):
                if b + 1 < B:
                    pe.wait_ge(s_dot, N * GROUPS + b + 1)
                    spread_h2(b + 1)
                pe.wait_ge(s_dg, N * GROUPS + b + 1)
                for half in range(2):
                    last = pe.matmul(psS[0][0:B, half * 512:half * 512 + 512], coef[:, b, :],
                                     ring[b][:, D + half * 512:D + half * 512 + 512],
                                     start=(b == 0), stop=(b == B - 1), skip_group_check=True)
            last.then_inc(s_y, 1)

        @block.vector
        def _(dve):
            steps = [0]

            def step(ins):
                steps[0] += 1
                ins.then_inc(s_ch, 1)
                dve.wait_ge(s_ch, steps[0])

            def restart():
                dve.sem_clear(s_ch)
                steps[0] = 0

            def best8(r, m, ix, values, n):
                step(dve.max(m[:, 0:8], values))
                step(dve.match_replace(work[0:r, 0:n], m[:, 0:8], values, LOWEST))
                step(dve.max_index(ix[:, 0:8], m[:, 0:8], values))

            def next8(r, m, ix, n):
                step(dve.max(m[:, 8:16], work[0:r, 0:n]))
                step(dve.max_index(ix[:, 8:16], m[:, 8:16], work[0:r, 0:n]))

            def choose(part, r, scores, delta, expert_f):
                if part in (1, 2):
                    c = part - 1
                    best8(r, top[0:r, c, :], pos[0:r, c, :], scores[:, c * NK:(c + 1) * NK], NK)
                    next8(r, top[0:r, c, :], pos[0:r, c, :], NK)
                if part == 3:
                    step(dve.tensor_tensor(cand[0:r], top[0:r, 0, :].unsqueeze(2).to_broadcast([r, TOPK, TOPK]),
                                           top[0:r, 1, :].unsqueeze(1).to_broadcast([r, TOPK, TOPK]), ALU.add))
                    best8(r, top[0:r, 2, :], pos[0:r, 2, :], cand[0:r].rearrange("p a b -> p (a b)"), TOPK * TOPK)
                if part == 4:
                    next8(r, top[0:r, 2, :], pos[0:r, 2, :], TOPK * TOPK)
                    step(dve.tensor_scalar(half_pos[0:r, 0, :], pos[0:r, 2, :], 4, None, ALU.logical_shift_right))
                    step(dve.tensor_scalar(half_pos[0:r, 1, :], pos[0:r, 2, :], TOPK - 1, None, ALU.bitwise_and))
                    step(dve.tensor_copy(half_f[0:r], half_pos[0:r]))
                    step(dve.tensor_copy(key_f[0:r], pos[0:r, 0:2, :]))
                if part in (5, 6):
                    c = part - 5
                    step(dve.tensor_tensor(hit[0:r], half_f[0:r, c, :].unsqueeze(2).to_broadcast([r, TOPK, TOPK]),
                                           iota[0:r].unsqueeze(1).to_broadcast([r, TOPK, TOPK]), ALU.is_equal))
                    step(dve.tensor_tensor(hit[0:r], hit[0:r],
                                           key_f[0:r, c, :].unsqueeze(1).to_broadcast([r, TOPK, TOPK]), ALU.mult))
                    step(dve.tensor_reduce(pick[0:r, c, :], hit[0:r], AX, ALU.add))
                if part == 7:
                    step(dve.tensor_scalar(delta[:], top[0:r, 2, :], top[0:r, 2, 0:1], None, ALU.subtract))
                    step(dve.scalar_tensor_tensor(out=expert_f[:], in0=pick[0:r, 0, :], scalar=float(NK),
                                                  in1=pick[0:r, 1, :], op0=ALU.mult, op1=ALU.add))

            def choose_next(part, n, u):
                if part == 1:
                    dve.wait_ge(s_scc, n + 2)
                    dve.sem_inc(s_passed, 1)
                choose(part, P, sc[u], delta[u], expert_f[u])
                if part == 2:
                    dve.sem_inc(s_scu, 1)
                if part == 7:
                    dve.tensor_copy(expert[u][:], expert_f[u][:]).then_inc(s_top, 1)

            PARTS = 8
            assert PARTS == GROUPS
            dve.memset(zeros[:], 0.0).then_inc(s_set, 1)
            dve.memset(coef[:], 0.0).then_inc(s_set, 1)
            dve.memset(qT_s[:], 0.0).then_inc(s_set, 1)
            dve.memset(gsum_s[:], 0.0).then_inc(s_free, RING // GRP)
            dve.wait_ge(s_w, 48)
            for n in range(2):
                for part in range(PARTS):
                    choose_next(part, n, n)
            dve.wait_ge(s_sa, 4)
            for part in range(PARTS):
                choose(part, ROWS_S, sc_s, delta_s, expert_s)
            dve.sem_inc(s_tops, 1)
            dve.sem_inc(s_gts, 1)
            dve.wait_ge(s_ges, 1)
            step(dve.reciprocal(gsum_s[:, 1:2], gsum_s[:, 0:1]))
            dve.tensor_scalar(gate_s[:], gate_s[:], gsum_s[:, 1:2], None, ALU.mult).then_inc(s_gts, 1)

            with dve.Fori(0, T) as t:
                dve.wait_ge(s_h2, t * 16 + 16)
                dve.wait_ge(s_hT, t * 2 + 2)
                dve.tensor_copy(h2cur[:], h2next[:]).then_inc(s_cur, 1)
                dve.wait_ge(s_cur, t + 1)
                dve.sem_inc(s_passed, 1)
                with dve.Fori(0, PAIRS) as pair:
                    for u in range(2):
                        n = t * HP + pair * 2 + u
                        restart()
                        for q in range(GROUPS):
                            for s in range(q * GRP, q * GRP + GRP):
                                r = s % RING
                                dve.wait_ge(s_g[r], (n * (TOPK // RING) + s // RING) * 16 + 16)
                                last = dve.tensor_tensor_reduce(ring[r][:, 0:D], ring[r][:, 0:D], h2cur[:], 1.0, 0.0,
                                                                ALU.mult, ALU.add, dot[:, s:s + 1])
                            last.then_inc(s_dot, 1)
                            if q == 0:
                                dve.wait_ge(s_ge, n + 1)
                                step(dve.reciprocal(gsum[u][:, 1:2], gsum[u][:, 0:1]))
                            dve.wait_ge(s_gelu, n * GROUPS + q + 1)
                            c = slice(q * GRP, q * GRP + GRP)
                            dve.scalar_tensor_tensor(out=act_h[:, c], in0=act_h[:, c], scalar=gsum[u][:, 1:2],
                                                     in1=gate_h[u][:, c], op0=ALU.mult, op1=ALU.mult)\
                               .then_inc(s_coef, 1)
                            dve.wait_ge(s_coef, n * GROUPS + q + 1)
                            for s in range(q * GRP, q * GRP + GRP):
                                last = dve.tensor_scalar(diag[:, s, :], ident[:], act_h[:, s:s + 1], None, ALU.mult)
                            last.then_inc(s_dg, 1)
                            choose_next(q, n + 2, u)
                restart()
                dve.wait_ge(s_yc, t + 2)
                dve.wait_ge(s_xm, t * 16 + 16)
                step(dve.tensor_tensor(ysum[:], ysum[:], gt2row[:], ALU.mult))
                dve.tensor_tensor(ysum[:], ysum[:], xmid[:], ALU.add).then_inc(s_out, 1)
            restart()
            for b in range(B + 1):
                if b < B:
                    dve.wait_ge(s_g[b], N * (TOPK // RING) * 16 + 16)
                    dve.wait_ge(s_bc, b + 1)
                    dve.tensor_tensor_reduce(ring[b][:, 0:D], ring[b][:, 0:D], psS[1][:], 1.0, 0.0,
                                             ALU.mult, ALU.add, dot[:, b:b + 1]).then_inc(s_dot, 1)
                if b == 0:
                    dve.wait_ge(s_xl, 32 * HP)
                if b >= 1:
                    c = b - 1
                    dve.wait_ge(s_gelu, N * GROUPS + c + 1)
                    dve.tensor_scalar(coef[:, c, c:c + 1], act_h[:, c:c + 1], gateT[:, c:c + 1], None, ALU.mult)\
                       .then_inc(s_dg, 1)
            dve.wait_ge(s_y, T + 1)
            step(dve.tensor_tensor(y_s[:], psS[0][0:B, :], gt2s[:], ALU.mult))
            dve.tensor_tensor(y_s[:], y_s[:], xmid_s[:], ALU.add).then_inc(s_out, 1)


def _constants():
    f = np.float64
    c = {"c_ident": np.eye(P)}
    c["c_iota"] = np.tile(np.arange(TOPK, dtype=f), (P, 1))

    c["c_spread"] = np.repeat(np.eye(B)[:, :, None], P, axis=2)

    def counts(d):
        inside = [(d >= 0) & (d <= window) & (d % dil == 0) for window, dil in BRANCHES]
        return np.sum(inside, axis=0).astype(f)

    p, col = np.arange(P)[:, None], np.arange(SPAN)[None, :]
    d = p + (T - 1) * P - col
    c["c_dist"] = np.where(counts(d) > 0, -d, MASKED)
    d = (T - 1 - col // P) * P + col % P - p
    c["c_count"] = counts(d)
    log_decay = np.log1p(-np.exp2(-5.0 - np.arange(H, dtype=f)))
    i = np.arange(P)
    diff = i[None, :] - i[:, None]
    c["c_intra"] = np.concatenate([np.where(diff >= 0, np.exp(np.maximum(diff, 0) * g), 0) * HD ** -0.5
                                   for g in np.concatenate([log_decay[0::2], log_decay[1::2]])], axis=1)
    pair = np.exp((i + 1)[None, None, :] * log_decay.reshape(G, 2, 1))
    c["c_wstart"] = np.repeat(pair.transpose(1, 0, 2), HD, axis=0).reshape(P, G * P)
    c["c_wend"] = np.exp((P - 1 - i)[:, None] * log_decay[None, :]) * HD ** -0.5
    c["c_cdecay"] = np.repeat(np.exp(P * log_decay).reshape(G, 2).T, HD, axis=0)
    slopes = np.exp2(-(np.arange(H) + 1.0))
    c["c_qkscale"] = np.tile(np.concatenate([HD ** -0.5 / slopes, np.ones(H)]), (P, 1))
    age = np.array(_selected_ages() + [0])
    c["c_bias_s"] = np.tile(-slopes[:, None] * age[None, :], (B, 1))
    c["c_count_s"] = np.tile(counts(age)[None, :], (B * H, 1))
    c["c_gamma"] = np.tile(np.exp(log_decay)[:, None], (B, 1))
    return {k: np.ascontiguousarray(v, np.float32) for k, v in c.items()}


def _selected_ages():
    ages = [g for g in range(1, PAST + 1) if any(g <= w and g % d == 0 for w, d in BRANCHES)]
    assert len(ages) == NSEL
    return ages


def _layout(x):
    z = {k: np.asarray(v) for k, v in x.items()}
    r = {"x_sample": z["x_sample"][:, 0]}
    r["x_all"] = np.concatenate([z["x_prompt"][0], np.zeros((P, D), np.float32)])
    c = np.concatenate([z["c_sample"], z["c_prompt"]], axis=0).T
    r["cT"] = c.reshape(KT, P, NC9).transpose(1, 0, 2)
    for n in ("w_ada", "w_in", "w_out", "w_pq"):
        r[n] = z[n][0]
    r["b_adaT"] = z["b_ada"][0].reshape(48, P).T
    r["gnT"] = np.stack([z["g_norm1"][0].reshape(KT, P).T, z["g_norm2"][0].reshape(KT, P).T], axis=1)
    r["g_qk"] = np.tile(np.concatenate([z["g_qn"][0].reshape(-1), z["g_kn"][0].reshape(-1)]), (P, 1))
    keys = np.zeros((P, HP, 2 * NK), np.float32)
    for c in range(2):
        keys[c * HD:(c + 1) * HD, :, c * NK:(c + 1) * NK] = z["sub_keys"][0, :, c].transpose(2, 0, 1)
    r["subk"] = keys
    r["uv"] = np.concatenate([z["peer_u"][0], z["peer_v"][0]], axis=1)
    r["state_s"] = z["state_ret"][0].reshape(B * H, HD, HD)
    rows = PAST - np.array(_selected_ages())
    r["k_sel"] = z["cache_win_k"][0][:, rows].transpose(0, 2, 1, 3).reshape(B * H, NSEL * HD)
    r["v_sel"] = z["cache_win_v"][0][:, rows].transpose(0, 2, 3, 1).reshape(B * H, HD * NSEL)
    r["g_qk_s"] = np.tile(np.stack([z["g_qn"][0], z["g_kn"][0]], axis=1), (B, 1, 1))
    r["g_ret_s"] = np.tile(z["g_ret"][0], (B, 1))
    r["g_ret_rows"] = np.tile(z["g_ret"][0].reshape(-1), (P, 1))
    return r


_OUTS = {"y_prompt": (1024, D), "y_sample": (B, D), "ret_prompt": (H * HD, HD), "wk_prompt": (1024, HW),
         "wv_prompt": (1024, HW), "ret_sample": (B * H, HD * HD), "wk_sample": (B * H, HD), "wv_sample": (B * H, HD)}
_SCRATCH = {"x_mid": ((T + 1) * P, D), "h2": ((T + 1) * P, D), "gt2_sample": (B, D),
            "expert_s": (HP, B, TOPK), "gate_s": (HP, B, TOPK), "proj_s": (NPROJ, B, HW), "mix_s": (B * H, 2 * HD)}


def kernel(**inputs):
    import concourse.bacc as bacc
    from concourse.bass_utils import run_bass_kernel_spmd as run

    nc = bacc.Bacc("TRN2", target_bir_lowering=False, num_devices=1)
    arrays, aps = {}, {}
    for name, v in {**_layout(inputs), **_constants()}.items():
        arrays[name] = np.ascontiguousarray(v)
        aps[name] = nc.dram_tensor(name, v.shape, F32, kind="ExternalInput").ap()
    for name, shape in _OUTS.items():
        aps[name] = nc.dram_tensor(name, shape, F32, kind="ExternalOutput").ap()
    for name, shape in _SCRATCH.items():
        aps[name] = nc.dram_tensor(name, shape, F32, kind="Internal").ap()
    build(nc, aps)
    got = run(nc, [arrays], core_ids=[0]).results[0]
    hd = (H, HD)
    return (got["y_prompt"].reshape(1, 1024, D), got["y_sample"].reshape(B, 1, D),
            got["ret_prompt"].reshape(1, 1, H, HD, HD), got["wk_prompt"].reshape(1, 1, 1024, *hd),
            got["wv_prompt"].reshape(1, 1, 1024, *hd), got["ret_sample"].reshape(1, B, H, HD, HD),
            got["wk_sample"].reshape(1, B, 1, *hd), got["wv_sample"].reshape(1, B, 1, *hd))
```
